# Optimizing a Trainium2 kernel written in Bass

```python
import jax, jax.numpy as jnp
from jax import lax
import numpy as np
import math

D_MODEL = 1024
BATCH = 1
SEQ = 256
DEPTH = 1

CONV_CH = D_MODEL
CONV_WIDTH = 31
HEAD_DIM = 64
N_Q_HEADS = 16
N_KV_HEADS = 2
GROUP = N_Q_HEADS // N_KV_HEADS
ATTN_W = N_Q_HEADS * HEAD_DIM
KV_W = N_KV_HEADS * HEAD_DIM
WINDOW = 128
BLOCK = 128
ROPE_THETA = 10000.0
PEER_HEADS = 8
N_KEYS = 128
N_EXPERTS = N_KEYS * N_KEYS
PEER_DKEY = 256
PEER_DHALF = PEER_DKEY // 2
PEER_TOPK = 16
PEER_CHUNK = 128
IN_COLS = 2 * CONV_CH + ATTN_W + 2 * KV_W + 2 * D_MODEL
EPS = 1e-6
NEG = -1e30


def rmsnorm(x, g):
    xf = x.astype(jnp.float32)
    y = xf * lax.rsqrt(jnp.mean(xf * xf, axis=-1, keepdims=True) + EPS)
    return (y * g.astype(jnp.float32)).astype(x.dtype)

def layernorm(x, g, b):
    xf = x.astype(jnp.float32)
    mu = jnp.mean(xf, axis=-1, keepdims=True)
    xc = xf - mu
    y = xc * lax.rsqrt(jnp.mean(xc * xc, axis=-1, keepdims=True) + EPS)
    return (y * g.astype(jnp.float32) + b.astype(jnp.float32)).astype(x.dtype)

def rope(t, positions):
    half = HEAD_DIM // 2
    inv = ROPE_THETA ** (-(jnp.arange(half, dtype=jnp.float32) * 2.0 / HEAD_DIM))
    ang = positions.astype(jnp.float32)[..., None] * inv
    cos = jnp.cos(ang)[:, :, None, :]
    sin = jnp.sin(ang)[:, :, None, :]
    tf = t.astype(jnp.float32)
    t1, t2 = tf[..., :half], tf[..., half:]
    out = jnp.concatenate([t1 * cos - t2 * sin, t2 * cos + t1 * sin], axis=-1)
    return out.astype(t.dtype)

def conformer_conv(val, gate, conv_w, conv_b, ln_g, ln_b, w_conv_out):
    u = val * jax.nn.sigmoid(gate)
    up = jnp.pad(u, ((0, 0), (CONV_WIDTH - 1, 0), (0, 0)))
    y = lax.conv_general_dilated(
        up, conv_w[:, None, :], window_strides=(1,), padding="VALID",
        dimension_numbers=("NWC", "WIO", "NWC"), feature_group_count=CONV_CH) + conv_b
    y = jax.nn.silu(layernorm(y, ln_g, ln_b))
    return y @ w_conv_out

def swa_sink_attention(q, k, v, sinks):
    B, S = q.shape[0], q.shape[1]
    nb = S // BLOCK
    qb = q.reshape(B, nb, BLOCK, N_KV_HEADS, GROUP, HEAD_DIM)

    def band(t):
        tp = jnp.pad(t, ((0, 0), (BLOCK, 0), (0, 0), (0, 0)))
        tb = tp.reshape(B, nb + 1, BLOCK, N_KV_HEADS, HEAD_DIM)
        return jnp.concatenate([tb[:, :-1], tb[:, 1:]], axis=2)

    kb, vb = band(k), band(v)
    s = jnp.einsum("bnqhgd,bnkhd->bnhgqk", qb, kb,
                   preferred_element_type=jnp.float32) * (HEAD_DIM ** -0.5)
    qi = jnp.arange(BLOCK)[:, None]
    kj = jnp.arange(2 * BLOCK)[None, :]
    rel = qi + BLOCK - kj
    in_window = (rel >= 0) & (rel < WINDOW)
    not_pad = (kj >= BLOCK)[None] | (jnp.arange(nb)[:, None, None] > 0)
    mask = in_window[None] & not_pad
    s = jnp.where(mask[None, :, None, None], s, NEG)
    sk = sinks.astype(jnp.float32).reshape(N_KV_HEADS, GROUP)[:, :, None, None]
    m = jnp.maximum(jnp.max(s, axis=-1, keepdims=True), sk)
    e = jnp.exp(s - m)
    p = e / (jnp.sum(e, axis=-1, keepdims=True) + jnp.exp(sk - m))
    o = jnp.einsum("bnhgqk,bnkhd->bnqhgd", p.astype(v.dtype), vb)
    return o.reshape(B, S, ATTN_W)

def peer(h, w_pq, sub_keys, u_emb, v_emb):
    B, S, D = h.shape
    q = (h @ w_pq).reshape(B, S, PEER_HEADS, 2, PEER_DHALF)
    sc = jnp.einsum("bshcd,hcnd->bshcn", q, sub_keys,
                    preferred_element_type=jnp.float32)
    s_top, i_top = lax.top_k(sc, PEER_TOPK)
    cand = s_top[..., 0, :, None] + s_top[..., 1, None, :]
    cand_idx = i_top[..., 0, :, None] * N_KEYS + i_top[..., 1, None, :]
    cand = cand.reshape(B, S, PEER_HEADS, PEER_TOPK * PEER_TOPK)
    cand_idx = cand_idx.reshape(B, S, PEER_HEADS, PEER_TOPK * PEER_TOPK)
    best, pos = lax.top_k(cand, PEER_TOPK)
    expert_idx = jnp.take_along_axis(cand_idx, pos, axis=-1)
    gate = jax.nn.softmax(best, axis=-1).astype(h.dtype)

    n_chunks = (B * S) // PEER_CHUNK
    hc = h.reshape(n_chunks, PEER_CHUNK, D)
    ic = expert_idx.reshape(n_chunks, PEER_CHUNK, PEER_HEADS * PEER_TOPK)
    gc = gate.reshape(n_chunks, PEER_CHUNK, PEER_HEADS * PEER_TOPK)

    def chunk(args):
        hx, idx, g = args
        a = jax.nn.gelu(jnp.einsum("ced,cd->ce", u_emb[idx], hx), approximate=False)
        return jnp.einsum("ce,ced->cd", g * a, v_emb[idx])

    out = lax.map(chunk, (hc, ic, gc))
    return out.reshape(B, S, D)

def first_inputs(seed: int = 0) -> dict:
    key = jax.random.key(seed)
    ks = jax.random.split(key, 20)
    f32 = jnp.float32
    nrm = lambda k, shape, scale: jax.random.normal(k, shape, f32) * scale
    L = DEPTH
    return {
        "x": nrm(ks[0], (BATCH, SEQ, D_MODEL), 1.0),
        "positions": jnp.broadcast_to(jnp.arange(SEQ, dtype=jnp.int32)[None, :], (BATCH, SEQ)),
        "norm1_g": 1.0 + nrm(ks[1], (L, D_MODEL), 0.02),
        "w_in": nrm(ks[2], (L, D_MODEL, IN_COLS), D_MODEL ** -0.5),
        "b_in": nrm(ks[3], (L, IN_COLS), 0.01),
        "conv_w": nrm(ks[4], (L, CONV_WIDTH, CONV_CH), CONV_WIDTH ** -0.5),
        "conv_b": nrm(ks[5], (L, CONV_CH), 0.01),
        "conv_ln_g": 1.0 + nrm(ks[6], (L, CONV_CH), 0.02),
        "conv_ln_b": nrm(ks[7], (L, CONV_CH), 0.01),
        "w_conv_out": nrm(ks[8], (L, CONV_CH, D_MODEL), CONV_CH ** -0.5),
        "attn_sinks": nrm(ks[9], (L, N_Q_HEADS), 0.5),
        "w_attn_o": nrm(ks[10], (L, ATTN_W, D_MODEL), ATTN_W ** -0.5),
        "w_out": nrm(ks[11], (L, D_MODEL, D_MODEL), D_MODEL ** -0.5),
        "norm2_g": 1.0 + nrm(ks[12], (L, D_MODEL), 0.02),
        "w_peer_q": nrm(ks[13], (L, D_MODEL, PEER_HEADS * PEER_DKEY), D_MODEL ** -0.5),
        "peer_sub_keys": nrm(ks[14], (L, PEER_HEADS, 2, N_KEYS, PEER_DHALF), PEER_DHALF ** -0.5),
        "peer_u": nrm(ks[15], (L, N_EXPERTS, D_MODEL), D_MODEL ** -0.5),
        "peer_v": nrm(ks[16], (L, N_EXPERTS, D_MODEL), (PEER_HEADS * PEER_TOPK) ** -0.5),
        "final_g": 1.0 + nrm(ks[17], (D_MODEL,), 0.02),
    }

def first_block(x, positions, norm1_g, w_in, b_in, conv_w, conv_b, conv_ln_g, conv_ln_b,
              w_conv_out, attn_sinks, w_attn_o, w_out, norm2_g, w_peer_q, peer_sub_keys,
              peer_u, peer_v, final_g):
    B, S, _ = x.shape
    c0 = CONV_CH
    c1 = c0 + CONV_CH
    c2 = c1 + ATTN_W
    c3 = c2 + KV_W
    c4 = c3 + KV_W
    c5 = c4 + D_MODEL
    for l in range(DEPTH):
        h = rmsnorm(x, norm1_g[l])
        z = h @ w_in[l] + b_in[l]
        glu_val, glu_gate, q, k, v, g_conv, g_attn = jnp.split(z, [c0, c1, c2, c3, c4, c5], axis=-1)

        conv_out = conformer_conv(glu_val, glu_gate, conv_w[l], conv_b[l],
                                  conv_ln_g[l], conv_ln_b[l], w_conv_out[l])

        q = rope(q.reshape(B, S, N_Q_HEADS, HEAD_DIM), positions)
        k = rope(k.reshape(B, S, N_KV_HEADS, HEAD_DIM), positions)
        v = v.reshape(B, S, N_KV_HEADS, HEAD_DIM)
        attn_out = swa_sink_attention(q, k, v, attn_sinks[l]) @ w_attn_o[l]

        merged = jax.nn.sigmoid(g_conv) * conv_out + jax.nn.sigmoid(g_attn) * attn_out
        x = x + merged @ w_out[l]

        h2 = rmsnorm(x, norm2_g[l])
        x = x + peer(h2, w_peer_q[l], peer_sub_keys[l], peer_u[l], peer_v[l])
    return rmsnorm(x, final_g)


DEPTH_2 = 2

NEG_INF = -1e30
A_HEADS = 8
A_BRANCHES = ((128, 1), (512, 4), (2048, 16))
T5_BUCKETS = 32
T5_MAX_DIST = 1024
B_HEADS = 8
B_Q_RANK = 768
B_KV_RANK = 256
B_NOPE = 64
B_ROPE = 32
B_V = 64
ROPE_BASE = 10000.0
ATTN_BLOCK = 128
C_GROUPS = 8
C_GROUP_W = 64
C_CHUNK = 128
C_WIDTH = C_GROUPS * C_GROUP_W
D_HEADS = 8
GRID_W = 64
NA_ROWS = 8
NA_COLS = 16
FFN_HIDDEN = -(-8 * D_MODEL // (3 * 256)) * 256
A_WIDTH = A_HEADS * HEAD_DIM
D_WIDTH = D_HEADS * HEAD_DIM
EVEN_IN = 3 * A_WIDTH + B_Q_RANK + B_KV_RANK + B_ROPE
EVEN_MIX = A_WIDTH + B_HEADS * B_V
ODD_IN = 2 * C_WIDTH + 3 * D_WIDTH
ODD_MIX = C_WIDTH + D_WIDTH
N_EVEN = (DEPTH_2 + 1) // 2
N_ODD = DEPTH_2 // 2


def _rmsnorm(x, g):
    xf = x.astype(jnp.float32)
    y = xf * lax.rsqrt(jnp.mean(xf * xf, -1, keepdims=True) + EPS) * g.astype(jnp.float32)
    return y.astype(x.dtype)

def _t5_bucket(rel):
    nb = T5_BUCKETS // 2
    max_exact = nb // 2
    n = np.abs(rel)
    large = max_exact + (np.log(np.maximum(n, 1) / max_exact) / math.log(T5_MAX_DIST / max_exact) * (nb - max_exact)).astype(np.int64)
    large = np.minimum(large, nb - 1)
    return ((rel > 0) * nb + np.where(n < max_exact, n, large)).astype(np.int32)

def _dilated_branch(q, k, v, t5_table, window, dil):
    B, S, H, hd = q.shape
    half = (window // 2) // dil
    L = S // dil
    nb = -(-L // half)
    Lp = nb * half

    def sub(t):
        return t.reshape(B, L, dil, H, hd).transpose(0, 2, 1, 3, 4)

    qs = jnp.pad(sub(q), ((0, 0), (0, 0), (0, Lp - L), (0, 0), (0, 0))).reshape(B, dil, nb, half, H, hd)

    def win(t):
        tp = jnp.pad(sub(t), ((0, 0), (0, 0), (half, Lp - L + half), (0, 0), (0, 0))).reshape(B, dil, nb + 2, half, H, hd)
        return jnp.concatenate([tp[:, :, 0:nb], tp[:, :, 1:nb + 1], tp[:, :, 2:nb + 2]], axis=3)

    kw, vw = win(k), win(v)
    qi = np.arange(half)[:, None]
    kj = np.arange(3 * half)[None, :]
    off = kj - half - qi
    key_idx = np.arange(nb)[:, None, None] * half - half + kj[None]
    valid = (np.abs(off) <= half)[None] & (key_idx >= 0) & (key_idx < L)
    bias = jnp.transpose(t5_table[_t5_bucket(off * dil)], (2, 0, 1)).astype(jnp.float32)
    s = jnp.einsum('bgnqhd,bgnkhd->bgnhqk', qs, kw).astype(jnp.float32) * (hd ** -0.5) + bias
    s = jnp.where(valid[None, None, :, None], s, NEG_INF)
    m = jnp.max(s, -1, keepdims=True)
    p = jnp.exp(s - m)
    den = jnp.sum(p, -1)
    o = jnp.einsum('bgnhqk,bgnkhd->bgnqhd', p, vw.astype(jnp.float32)) / jnp.transpose(den, (0, 1, 2, 4, 3))[..., None]
    lse = m[..., 0] + jnp.log(den)
    o = o.reshape(B, dil, Lp, H, hd)[:, :, :L].transpose(0, 2, 1, 3, 4).reshape(B, S, H, hd)
    lse = jnp.transpose(lse, (0, 1, 2, 4, 3)).reshape(B, dil, Lp, H)[:, :, :L].transpose(0, 2, 1, 3).reshape(B, S, H)
    return o, lse

def _dilated_mixture(q, k, v, t5_table):
    B, S, H, hd = q.shape
    outs, lses = zip(*[_dilated_branch(q, k, v, t5_table, w, d) for (w, d) in A_BRANCHES])
    wts = jax.nn.softmax(jnp.stack(lses, 0), axis=0)
    o = jnp.sum(wts[..., None] * jnp.stack(outs, 0), 0)
    return o.astype(q.dtype).reshape(B, S, H * hd)

def _rope_tables(S):
    pos = jnp.arange(S, dtype=jnp.float32)
    inv = 1.0 / (ROPE_BASE ** (jnp.arange(0, B_ROPE, 2, dtype=jnp.float32) / B_ROPE))
    ang = pos[:, None] * inv[None, :]
    return jnp.cos(ang), jnp.sin(ang)

def _apply_rope(x, cos, sin):
    hf = B_ROPE // 2
    shape = (1, x.shape[1]) + (1,) * (x.ndim - 3) + (hf,)
    c, s = cos.reshape(shape), sin.reshape(shape)
    xf = x.astype(jnp.float32)
    x1, x2 = xf[..., :hf], xf[..., hf:]
    return jnp.concatenate([x1 * c - x2 * s, x1 * s + x2 * c], -1).astype(x.dtype)

def _mla(c_q, c_kv, k_pe, q_gain, kv_gain, w_uq, w_ukv, cos, sin):
    B, S, _ = c_q.shape
    q = (_rmsnorm(c_q, q_gain) @ w_uq).reshape(B, S, B_HEADS, B_NOPE + B_ROPE)
    kv = (_rmsnorm(c_kv, kv_gain) @ w_ukv).reshape(B, S, B_HEADS, B_NOPE + B_V)
    q = jnp.concatenate([q[..., :B_NOPE], _apply_rope(q[..., B_NOPE:], cos, sin)], -1)
    k_pe = _apply_rope(k_pe, cos, sin)
    k = jnp.concatenate([kv[..., :B_NOPE], jnp.broadcast_to(k_pe[:, :, None, :], (B, S, B_HEADS, B_ROPE))], -1)
    v = kv[..., B_NOPE:]
    scale = (B_NOPE + B_ROPE) ** -0.5
    nq = S // ATTN_BLOCK
    qb = q.reshape(B, nq, ATTN_BLOCK, B_HEADS, B_NOPE + B_ROPE).transpose(1, 0, 2, 3, 4)

    def block(qblk):
        s = jnp.einsum('bqhd,bkhd->bhqk', qblk, k).astype(jnp.float32) * scale
        p = jax.nn.softmax(s, -1)
        return jnp.einsum('bhqk,bkhd->bqhd', p, v.astype(jnp.float32)).astype(v.dtype)

    o = lax.map(block, qb)
    return o.transpose(1, 0, 2, 3, 4).reshape(B, S, B_HEADS * B_V)

def _spatial_gating(z_in, v_gain, w_s, b_s):
    B, S, _ = z_in.shape
    z = jax.nn.gelu(z_in.astype(jnp.float32))
    u, v = z[..., :C_WIDTH], z[..., C_WIDTH:]
    mu = jnp.mean(v, -1, keepdims=True)
    var = jnp.mean((v - mu) ** 2, -1, keepdims=True)
    vn = (v - mu) * lax.rsqrt(var + EPS) * v_gain.astype(jnp.float32)
    vc = vn.reshape(B, S // C_CHUNK, C_CHUNK, C_GROUPS, C_GROUP_W)
    sv = jnp.einsum('gij,bnjgc->bnigc', w_s.astype(jnp.float32), vc) + jnp.transpose(b_s.astype(jnp.float32))[None, None, :, :, None]
    return (u * sv.reshape(B, S, C_WIDTH)).astype(z_in.dtype)

def _neighbourhood_attention(q, k, v, rpb):
    B, S, H, hd = q.shape
    rows = S // GRID_W
    kr = min(NA_ROWS, rows)
    n_cb = GRID_W // NA_COLS
    kcw = 2 * NA_COLS
    qcol = np.arange(GRID_W).reshape(n_cb, NA_COLS)
    qstart = np.clip(qcol - NA_COLS // 2, 0, GRID_W - NA_COLS)
    kb_start = np.clip(np.arange(n_cb) * NA_COLS - NA_COLS // 2, 0, GRID_W - kcw)
    kcol = kb_start[:, None] + np.arange(kcw)[None, :]
    col_mask = (kcol[:, None, :] >= qstart[..., None]) & (kcol[:, None, :] < qstart[..., None] + NA_COLS)
    dc = np.clip(kcol[:, None, :] - qcol[..., None] + NA_COLS - 1, 0, 2 * NA_COLS - 2)
    qg = q.reshape(B, rows, GRID_W, H, hd)
    kg = k.reshape(B, rows, GRID_W, H, hd)
    vg = v.reshape(B, rows, GRID_W, H, hd)
    scale = hd ** -0.5

    def row_fn(args):
        qr, i = args
        r0 = jnp.clip(i - kr // 2, 0, rows - kr)
        krows = lax.dynamic_slice_in_dim(kg, r0, kr, axis=1)
        vrows = lax.dynamic_slice_in_dim(vg, r0, kr, axis=1)
        kblk = jnp.stack([krows[:, :, int(s0):int(s0) + kcw] for s0 in kb_start], axis=2)
        vblk = jnp.stack([vrows[:, :, int(s0):int(s0) + kcw] for s0 in kb_start], axis=2)
        qb = qr.reshape(B, n_cb, NA_COLS, H, hd)
        s = jnp.einsum('bcqhd,bacmhd->bhcqam', qb, kblk).astype(jnp.float32) * scale
        dr = r0 + jnp.arange(kr) - i + NA_ROWS - 1
        bias = rpb[:, dr[:, None, None, None], dc[None]].astype(jnp.float32)
        s = s + jnp.transpose(bias, (0, 2, 3, 1, 4))[None]
        s = jnp.where(col_mask[:, :, None, :], s, NEG_INF)
        p = jax.nn.softmax(s.reshape(B, H, n_cb, NA_COLS, kr * kcw), -1).reshape(s.shape)
        o = jnp.einsum('bhcqam,bacmhd->bcqhd', p, vblk.astype(jnp.float32))
        return o.reshape(B, GRID_W, H, hd).astype(q.dtype)

    out = lax.map(row_fn, (qg.transpose(1, 0, 2, 3, 4), jnp.arange(rows, dtype=jnp.int32)))
    return out.transpose(1, 0, 2, 3, 4).reshape(B, S, H * hd)

def second_inputs(seed: int = 0) -> dict:
    key = jax.random.key(seed)
    ks = jax.random.split(key, 20)

    def nrm(k, shape, scale):
        return jax.random.normal(k, shape, jnp.float32) * scale

    def gain(k, shape):
        return 1.0 + 0.05 * jax.random.normal(k, shape, jnp.float32)

    return {
        'x': nrm(ks[0], (BATCH, SEQ, D_MODEL), 1.0),
        't5_bias': nrm(ks[1], (T5_BUCKETS, A_HEADS), 0.2),
        'norm_mix': gain(ks[2], (DEPTH_2, D_MODEL)),
        'norm_ffn': gain(ks[3], (DEPTH_2, D_MODEL)),
        'ev_w_in': nrm(ks[4], (N_EVEN, D_MODEL, EVEN_IN), D_MODEL ** -0.5),
        'ev_q_gain': gain(ks[5], (N_EVEN, B_Q_RANK)),
        'ev_kv_gain': gain(ks[6], (N_EVEN, B_KV_RANK)),
        'ev_w_uq': nrm(ks[7], (N_EVEN, B_Q_RANK, B_HEADS * (B_NOPE + B_ROPE)), B_Q_RANK ** -0.5),
        'ev_w_ukv': nrm(ks[8], (N_EVEN, B_KV_RANK, B_HEADS * (B_NOPE + B_V)), B_KV_RANK ** -0.5),
        'ev_w_out': nrm(ks[9], (N_EVEN, EVEN_MIX, D_MODEL), EVEN_MIX ** -0.5),
        'od_w_in': nrm(ks[10], (N_ODD, D_MODEL, ODD_IN), D_MODEL ** -0.5),
        'od_v_gain': gain(ks[11], (N_ODD, C_WIDTH)),
        'od_w_s': nrm(ks[12], (N_ODD, C_GROUPS, C_CHUNK, C_CHUNK), C_CHUNK ** -0.5),
        'od_b_s': nrm(ks[13], (N_ODD, C_GROUPS, C_CHUNK), 0.1),
        'od_rpb': nrm(ks[14], (N_ODD, D_HEADS, 2 * NA_ROWS - 1, 2 * NA_COLS - 1), 0.2),
        'od_w_out': nrm(ks[15], (N_ODD, ODD_MIX, D_MODEL), ODD_MIX ** -0.5),
        'ffn_w_gu': nrm(ks[16], (DEPTH_2, D_MODEL, 2 * FFN_HIDDEN), D_MODEL ** -0.5),
        'ffn_w_down': nrm(ks[17], (DEPTH_2, FFN_HIDDEN, D_MODEL), FFN_HIDDEN ** -0.5),
        'final_gain': gain(ks[18], (D_MODEL,)),
    }

def second_block(x, t5_bias, norm_mix, norm_ffn, ev_w_in, ev_q_gain, ev_kv_gain, ev_w_uq, ev_w_ukv, ev_w_out,
              od_w_in, od_v_gain, od_w_s, od_b_s, od_rpb, od_w_out, ffn_w_gu, ffn_w_down, final_gain):
    B, S, _ = x.shape
    cos, sin = _rope_tables(S)
    for layer in range(DEPTH_2):
        h = _rmsnorm(x, norm_mix[layer])
        j = layer // 2
        if layer % 2 == 0:
            p = h @ ev_w_in[j]
            qa, ka, va = [p[..., i * A_WIDTH:(i + 1) * A_WIDTH].reshape(B, S, A_HEADS, HEAD_DIM) for i in range(3)]
            o0 = 3 * A_WIDTH
            o1 = o0 + B_Q_RANK
            o2 = o1 + B_KV_RANK
            a_out = _dilated_mixture(qa, ka, va, t5_bias)
            b_out = _mla(p[..., o0:o1], p[..., o1:o2], p[..., o2:o2 + B_ROPE], ev_q_gain[j], ev_kv_gain[j],
                         ev_w_uq[j], ev_w_ukv[j], cos, sin)
            x = x + jnp.concatenate([a_out, b_out], -1) @ ev_w_out[j]
        else:
            p = h @ od_w_in[j]
            c_out = _spatial_gating(p[..., :2 * C_WIDTH], od_v_gain[j], od_w_s[j], od_b_s[j])
            base = 2 * C_WIDTH
            qd, kd, vd = [p[..., base + i * D_WIDTH:base + (i + 1) * D_WIDTH].reshape(B, S, D_HEADS, HEAD_DIM) for i in range(3)]
            d_out = _neighbourhood_attention(qd, kd, vd, od_rpb[j])
            x = x + jnp.concatenate([c_out, d_out], -1) @ od_w_out[j]
        h = _rmsnorm(x, norm_ffn[layer])
        gu = h @ ffn_w_gu[layer]
        x = x + (jax.nn.silu(gu[..., :FFN_HIDDEN]) * gu[..., FFN_HIDDEN:]) @ ffn_w_down[layer]
    return _rmsnorm(x, final_gain)


def setup_inputs(seed=0):
    out = dict(first_inputs(seed))
    for name, value in second_inputs(seed + 1).items():
        if name != "x":
            out[name + "_2"] = value
    return out


def reference(
    x, positions, norm1_g, w_in, b_in, conv_w, conv_b, conv_ln_g, conv_ln_b, w_conv_out,
    attn_sinks, w_attn_o, w_out, norm2_g, w_peer_q, peer_sub_keys, peer_u, peer_v, final_g,
    t5_bias_2, norm_mix_2, norm_ffn_2, ev_w_in_2, ev_q_gain_2, ev_kv_gain_2, ev_w_uq_2,
    ev_w_ukv_2, ev_w_out_2, od_w_in_2, od_v_gain_2, od_w_s_2, od_b_s_2, od_rpb_2, od_w_out_2,
    ffn_w_gu_2, ffn_w_down_2, final_gain_2,
):
    x = first_block(
        x, positions, norm1_g, w_in, b_in, conv_w, conv_b, conv_ln_g, conv_ln_b, w_conv_out,
        attn_sinks, w_attn_o, w_out, norm2_g, w_peer_q, peer_sub_keys, peer_u, peer_v, final_g,
    )
    return second_block(
        x, t5_bias_2, norm_mix_2, norm_ffn_2, ev_w_in_2, ev_q_gain_2, ev_kv_gain_2, ev_w_uq_2,
        ev_w_ukv_2, ev_w_out_2, od_w_in_2, od_v_gain_2, od_w_s_2, od_b_s_2, od_rpb_2,
        od_w_out_2, ffn_w_gu_2, ffn_w_down_2, final_gain_2,
    )


_drawn_inputs = setup_inputs


def setup_inputs(seed=0):
    import zlib

    import numpy as np

    out = dict(_drawn_inputs(seed))
    spreads = {}
    factors = {'norm1_g': 4.324,
     'b_in': 4.383,
     'conv_b': 4.617,
     'conv_ln_g': 4.307,
     'conv_ln_b': 8.0,
     'attn_sinks': 6.766,
     'norm2_g': 6.694,
     'ev_q_gain_2': 8.0,
     'ev_kv_gain_2': 5.526,
     'od_v_gain_2': 9.717,
     't5_bias_2': 8.0,
     'norm_ffn_2': 3.544,
     'od_b_s_2': 4.91,
     'od_rpb_2': 8.0}
    for name, (base, spread) in spreads.items():
        noise = np.random.default_rng([zlib.crc32(name.encode()), seed]).standard_normal(out[name].shape)
        drawn = base * np.exp(spread * noise) if base else spread * noise
        out[name] = __import__('jax').numpy.asarray(drawn.astype(out[name].dtype))
    for name, factor in factors.items():
        out[name] = (out[name] * factor).astype(out[name].dtype)
    return out
```

```python
from contextlib import ExitStack

import numpy as np
import concourse.bass as bass
from concourse import mybir

F32 = mybir.dt.float32
U32 = mybir.dt.uint32
I32 = mybir.dt.int32
ALU = mybir.AluOpType
ACT = mybir.ActivationFunctionType
AX = mybir.AxisListType.X

P = 128
S = 256
NT = S // P
D = 1024
KD = D // P
TAPS = 31
HD = 64
QH, KVH = 16, 2
PH, TOPK, NKEYS = 8, 16, 128
SLOTS = PH * TOPK
NEXP = NKEYS * NKEYS
FF = 2816
KF = FF // P
HEADS2 = 8
QRANK, KVRANK, NOPE, ROPE2 = 768, 256, 64, 32
QK2 = NOPE + ROPE2
CW = 512
GRID = 64
EPS = 1e-6
NEG = -1e30
NSLOT = 3
SLOTW = 4096
RB = 6
REL = 2 * S
TABW = S + P



def columns(parts):
    at, out = 0, {}
    for name, n in parts:
        out[name] = (at, at + n)
        at += n
    return out, at


CONST, NCONST = columns([("ident", 128), ("ones", 128), ("inv", 32), ("mask1", TABW), ("namask", GRID),
                         ("cos2", 32), ("sin2", 32), ("iota", 16)])
PARAM, NPARAM = columns([("norm1", 8), ("b_glu", 16), ("b_gate", 16), ("conv_w", KD * TAPS), ("conv_b", 8),
                         ("ln_g", 8), ("ln_b", 8), ("mix0", 8), ("mix1", 8), ("ffn0", 8), ("ffn1", 8),
                         ("qkv_gain", 8), ("b_s", 8)])
ROW, NROW = columns([("b_qkv", 1280), ("sinks", 16), ("norm2", D), ("final1", D)])
LATE = {"final2": (0, D), "v_gain": (1296, 1296 + CW)}
RPB_ROWS = 7



def chunk_list():
    out = [(("glu", i), 4096) for i in range(4)] + [(("q1", i), 4096) for i in range(2)] + [(("kv1", 0), 2048)]
    out += [(("gate", i), 4096) for i in range(4)]
    out += [(("convout", i), 4096) for i in range(2)] + [(("attno", i), 4096) for i in range(2)]
    out += [(("wout", i), 4096) for i in range(2)]
    out += [(("pq", i), 4096) for i in range(4)] + [(("keys", 0), 2048)]
    out += [(("qa", 0), 4096), (("ka", 0), 4096), (("va", 0), 4096), (("cqkv", 0), 4096), (("cqkv", 1), 4096),
            (("kpe_uq", 0), 3328), (("uq_ukv", 0), 3584), (("evout", 0), 4096), (("evout", 1), 4096)]
    for layer in range(2):
        if layer:
            out += [(("uz", 0), 4096), (("vz", 0), 4096), (("qd", 0), 4096), (("kd", 0), 4096), (("vd", 0), 4096),
                    (("ws", 0), 1024), (("odout", 0), 4096), (("odout", 1), 4096)]
        out += [(("gu%d" % layer, i), 4096) for i in range(KF // 2)]
        out += [(("down%d" % layer, i), min(4, KF - 4 * i) * D) for i in range(-(-KF // 4))]
    return out


CHUNKS = chunk_list()
CHUNK_NO = {name: n for n, (name, _) in enumerate(CHUNKS)}
CHUNK_AT = np.cumsum([0] + [P * w for _, w in CHUNKS]).tolist()



def attention_fills(a, heads):
    out = [(a, "S", 0), (a, "S", 1)]
    for h in range(heads):
        out.append((a, "T", h))
        if h + 2 < heads:
            out.append((a, "S", h + 2))
    return out + [(a, "OT", g, t) for g in range(heads // 8) for t in range(NT)]


def norm_fills(name):
    return [(name, t, half) for t in range(NT) for half in range(2)]


def tm_fills(name, chunks=1):
    return [(name, i, t) for i in range(chunks) for t in range(NT)]


def fm_fills(name, chunks=1):
    return [(name, i, pair) for i in range(chunks) for pair in range(2)]


def fill_list():
    out = [("t5",)] + norm_fills("N1") + fm_fills("glu", 4) + tm_fills("q1", 2) + tm_fills("kv1")
    out += fm_fills("gate", 4) + [("mean",), ("var",)]
    out += [("q1T", t, half) for t in range(NT) for half in range(2)] + [("k1T",)] + attention_fills("att1", QH)
    out += fm_fills("convout", 2) + fm_fills("attno", 2) + tm_fills("wout", 2)
    out += norm_fills("N2") + fm_fills("pq", 4) + [("sc", t, j) for t in range(NT) for j in range(4)]
    out += norm_fills("mix0") + fm_fills("qa") + fm_fills("ka") + tm_fills("va") + tm_fills("cqkv", 2)
    out += attention_fills("attA", HEADS2)
    out += norm_fills("cT") + tm_fills("kpe") + tm_fills("uqa") + tm_fills("uqb") + tm_fills("ukv", 2)
    out += [(n, t, half) for n in ("qmT", "kmT") for t in range(NT) for half in range(2)]
    out += attention_fills("attB", HEADS2) + tm_fills("evout", 2)
    for layer in range(2):
        if layer:
            out += norm_fills("mix1") + tm_fills("uz") + tm_fills("vz") + fm_fills("qd") + fm_fills("kd")
            out += tm_fills("vd") + [("gating", t) for t in range(NT)] + [("coutT", t) for t in range(NT)]
            out += attention_fills("attD", HEADS2) + tm_fills("odout", 2)
        out += norm_fills("ffn%d" % layer) + fm_fills("gu%d" % layer, KF // 2)
        out += [("down%d" % layer, half, t) for half in range(2) for t in range(NT)]
    return out


FILLS = fill_list()
FILL_NO = {name: n for n, name in enumerate(FILLS)}
assert len(FILL_NO) == len(FILLS)

LAST_USE = {("keys", 0): ("sc", 1, 3), ("kpe_uq", 0): ("uqa", 0, 1), ("uq_ukv", 0): ("ukv", 1, 1),
            ("ws", 0): ("gating", 1), ("down0", 5): ("down0", 1, 1), ("down1", 5): ("down1", 1, 1)}


def last_use(chunk):
    return LAST_USE.get(chunk, (chunk[0], chunk[1], 1))



class Attention:
    def __init__(self, name, heads, q, k, v, scale, table, sinks, column):
        self.name, self.heads, self.q, self.k, self.v = name, heads, q, k, v
        self.scale, self.table, self.sinks, self.column = scale, table, sinks, column


def build(nc, stream, consts, t5const, params, rows, late_rows, x_in, positions, t5_in, rpb_in, uv, out):
    with ExitStack() as ctx:
        def sb(name, shape, dt=F32):
            return ctx.enter_context(nc.sbuf_tensor(name, shape, dt))

        def sem(name):
            return ctx.enter_context(nc.semaphore(name))

        ring = sb("ring", [P, NSLOT, SLOTW])
        cst = sb("cst", [P, NCONST])
        par = sb("par", [P, NPARAM])
        row = sb("row", [P, NROW])
        x = sb("x", [P, NT, D])
        hT = sb("hT", [P, KD, S])
        xn = sb("xn", [P, NT, D])
        pool = sb("pool", [P, 16384])
        att = sb("att", [P, 7168])
        tab = sb("tab", [P, HEADS2, TABW])
        small = sb("small", [P, 64])
        ssq = small[:, 0:2]
        rstd = small[:, 32:36]
        eps = small[:, 4:5]
        posf = small[:, 6:8]
        nsink = small[:, 8:24]
        vsum = small[:, 24:26]
        pos_i = sb("pos_i", [P, NT], I32)
        nmax = sb("nmax", [P, QH, NT])
        den = sb("den", [P, QH, NT])
        sinkw = sb("sinkw", [P, QH, NT])
        kpe = sb("kpe", [P, NT, ROPE2])
        angles = sb("angles", [P, 4, NT, 32])
        topv = sb("topv", [P, 2 * PH, TOPK])
        topi = sb("topi", [P, 2 * PH, TOPK], U32)
        topf = sb("topf", [P, 2 * PH, TOPK])
        best = sb("best", [P, PH, TOPK])
        bpos = sb("bpos", [P, PH, TOPK], U32)
        bdig = sb("bdig", [P, 2, PH, TOPK], U32)
        bdigf = sb("bdigf", [P, 2, PH, TOPK])
        hits = sb("hits", [P, 2, PH, TOPK])
        gsum = sb("gsum", [P, PH])
        gates = sb("gates", [P, NT * SLOTS])
        experts = sb("experts", [P, NT * SLOTS], U32)
        stage = sb("stage", [P, 4, 2], U32)
        pause = sb("pause", [1, 2])
        dots = sb("dots", [P, 4, 2])
        acts = sb("acts", [P, 4, 2])
        coef = sb("coef", [P, 4, 2])

        def view(base, at, *shape):
            n = int(np.prod(shape))
            v = base[:, at:at + n]
            if len(shape) == 2:
                return v.rearrange("p (a b) -> p a b", a=shape[0])
            if len(shape) == 3:
                return v.rearrange("p (a b c) -> p a b c", a=shape[0], b=shape[1])
            return v

        def c_(name):
            return cst[:, CONST[name][0]:CONST[name][1]]

        def par_(name):
            return par[:, PARAM[name][0]:PARAM[name][1]]

        def row_(name):
            return row[:, ROW[name][0]:ROW[name][1]]

        ident, ones = c_("ident"), c_("ones")
        conv_w = par_("conv_w").rearrange("p (k w) -> p k w", k=KD)
        sc_sb = view(att, 0, 2, 512)
        pr_sb = view(att, 1024, 2, 512)
        pt_sb = view(att, 2048, 2, 512)
        otm = view(att, 3072, NT, D)
        oT = view(att, 5120, KD, S)
        rope_tmp = view(att, 3072, 4, 18, 32)
        u = view(pool, 0, KD, TAPS - 1 + S)
        y = view(pool, 2288, KD, S)
        sgc = view(pool, 4336, KD, S)
        sga = view(pool, 6384, KD, S)
        qkv = view(pool, 8432, NT, 1280)
        qkr = view(pool, 10992, NT, 18 * HD)
        q1T = view(pool, 13296, KD, S)
        k1T = view(pool, 15344, KVH, S)
        kdup = pool[:, 15856:16368].rearrange("p (t n c d) -> p t n c d", t=NT, n=KVH, c=2)
        glu_sig = view(pool, 13296, 2, 512)
        ysq = view(pool, 13296, KD, S)
        qpT = view(pool, 0, 2 * PH, S)
        gath = view(pool, 0, 8, 2 * D)
        scores = view(att, 0, NT, 2 * PH * NKEYS)
        cand = view(att, 4096, PH, TOPK * TOPK)
        qaT = view(pool, 0, 4, S)
        kaT = view(pool, 1024, 4, S)
        va = view(pool, 2048, NT, 512)
        cqkv = view(pool, 3072, NT, D)
        cT = view(pool, 5120, KD, S)
        uq = view(pool, 7168, NT, QRANK)
        ukv = view(pool, 8704, NT, D)
        km = view(pool, 10752, NT, HEADS2 * QK2)
        qmT = view(pool, 12288, HEADS2, S)
        kmT = view(pool, 14336, HEADS2, S)
        uz = view(pool, 0, NT, CW)
        vz = view(pool, 1024, NT, CW)
        qdT = view(pool, 2048, 4, S)
        kdT = view(pool, 3072, 4, S)
        vd = view(pool, 4096, NT, 512)
        cout = view(pool, 5120, NT, CW)
        guT = view(pool, 8192, KF, S)
        silu = view(pool, 13824, 2, 512)
        t5hot = att[0:32, 3072:3072 + REL]
        t5tab = att[0:32, 3584:3584 + HEADS2]
        t5ln = att[0:HEADS2, 3600:3600 + REL]
        t5vec = att[0:HEADS2, 4112:4112 + REL]
        rpb_pad = att[0:HEADS2, 4624:4624 + 15 * 128]

        t5_dram = nc.dram_tensor("t5_scratch", (HEADS2, P, REL), F32, kind="Internal").ap()
        rpb_dram = nc.dram_tensor("rpb_scratch", (HEADS2, RPB_ROWS, GRID, P), F32, kind="Internal").ap()

        psum = ctx.enter_context(nc.psum_tensor("psum", [P, 8, 512], F32))

        bank_filled = sem("bank_filled")
        bank_emptied = [sem("bank_emptied%d" % b) for b in range(RB)]
        chunk_landed = [sem("chunk_landed%d" % s) for s in range(NSLOT)]
        down_read = sem("down_read")
        const_landed = sem("const_landed")
        param_landed = sem("param_landed")
        x_landed = sem("x_landed")
        row_landed = sem("row_landed")
        pos_landed = sem("pos_landed")
        t5_landed = sem("t5_landed")
        rpb_landed = sem("rpb_landed")
        rpb_cleared = sem("rpb_cleared")
        t5_stored = sem("t5_stored")
        rpb_stored = sem("rpb_stored")
        taba_landed = sem("taba_landed")
        tabd_landed = sem("tabd_landed")
        tabd_ready = sem("tabd_ready")
        late_landed = sem("late_landed")
        vector_step = sem("vector_step")
        scalar_step = sem("scalar_step")
        eps_ready = sem("eps_ready")
        root_ready = sem("root_ready")
        x_normed = sem("x_normed")
        xn_ready = sem("xn_ready")
        angle_ready = sem("angle_ready")
        trig_ready = sem("trig_ready")
        conv_ready = sem("conv_ready")
        ysq_ready = sem("ysq_ready")
        ynorm_ready = sem("ynorm_ready")
        silu_ready = sem("silu_ready")
        rope_ready = sem("rope_ready")
        nmax_ready = sem("nmax_ready")
        probs_ready = sem("probs_ready")
        pv_done = sem("pv_done")
        nmaxs_ready = sem("nmaxs_ready")
        sinkw_ready = sem("sinkw_ready")
        o_emptied = sem("o_emptied")
        merged_ready = sem("merged_ready")
        shifted_ready = sem("shifted_ready")
        best_exp_ready = sem("best_exp_ready")
        selected = sem("selected")
        stage_ready = sem("stage_ready")
        rows_landed = [sem("rows_landed%d" % b) for b in range(4)]
        rows_used = sem("rows_used")
        dots_ready = sem("dots_ready")
        acts_ready = sem("acts_ready")
        vcen_ready = sem("vcen_ready")
        vroot_ready = sem("vroot_ready")
        vn_ready = sem("vn_ready")
        cout_ready = sem("cout_ready")
        out_ready = sem("out_ready")
        out_stored = sem("out_stored")

        def bank(name):
            return psum[:, FILL_NO[name] % RB, :]

        def wait_filled(eng, name):
            eng.wait_ge(bank_filled, FILL_NO[name] + 1)
            return bank(name)

        def emptied_sem(name):
            return bank_emptied[FILL_NO[name] % RB]

        def wait_emptied(eng, name):
            eng.wait_ge(emptied_sem(name), FILL_NO[name] // RB + 1)

        def wait_chunk(eng, name):
            n = CHUNK_NO[name]
            eng.wait_ge(chunk_landed[n % NSLOT], 16 * (n // NSLOT + 1))
            return ring[:, n % NSLOT, :]

        def half(h):
            return slice(HD * (h % 2), HD * (h % 2) + HD)

        def tile128(t):
            return slice(P * t, P * t + P)

        att1 = Attention(
            "att1", QH, lambda h, t: q1T[half(h), h // 2, tile128(t)], lambda h: k1T[half(h), h // (QH // KVH), :],
            lambda h, kt: qkv[:, kt, 1152 + HD * (h // 8):1152 + HD * (h // 8) + HD],
            HD ** -0.5, lambda h: c_("mask1"), True, lambda g: 512 * g)
        attA = Attention(
            "attA", HEADS2, lambda h, t: qaT[half(h), h // 2, tile128(t)], lambda h: kaT[half(h), h // 2, :],
            lambda h, kt: va[:, kt, HD * h:HD * h + HD], HD ** -0.5, lambda h: tab[:, h, :], False, lambda g: 0)
        attB = Attention(
            "attB", HEADS2, lambda h, t: qmT[0:QK2, h, tile128(t)], lambda h: kmT[0:QK2, h, :],
            lambda h, kt: ukv[:, kt, P * h + NOPE:P * h + P], QK2 ** -0.5, None, False, lambda g: 512)
        attD = Attention(
            "attD", HEADS2, lambda h, t: qdT[half(h), h // 2, tile128(t)], lambda h: kdT[half(h), h // 2, :],
            lambda h, kt: vd[:, kt, HD * h:HD * h + HD], HD ** -0.5, lambda h: tab[:, h, :], False, lambda g: 512)
        first_head = {"att1": 0, "attA": QH, "attB": QH + HEADS2, "attD": QH + 2 * HEADS2}
        gain_of = {"N1": "norm1", "mix0": "mix0", "mix1": "mix1", "ffn0": "ffn0", "ffn1": "ffn1", "cT": "qkv_gain"}
        first_probs = {"att1": 0, "attA": QH, "attD": QH + HEADS2}
        first_group = {"att1": 0, "attA": 2, "attB": 3, "attD": 4}

        def wait_probs(eng, a, h):
            if a.table is None:
                wait_emptied(eng, (a.name, "S", h))
            else:
                eng.wait_ge(probs_ready, first_probs[a.name] + h + 1)

        roots_before = {"N1": 0, "N2": 2, "F1": 4, "mix0": 6, "cT": 8, "ffn0": 12, "mix1": 14, "ffn1": 16, "F2": 18}
        xn_before = {"N1": 0, "N2": 2, "mix0": 4, "cT": 6, "ffn0": 8, "mix1": 10, "ffn1": 12}

        block = ctx.enter_context(nc.Block())

        @block.sync
        def _(sp):
            sp.dma_start(x[:, :, :], x_in.rearrange("(t p) d -> p t d", p=P)).then_inc(x_landed, 16)
            sp.dma_start(cst[:, :], consts).then_inc(const_landed, 16)
            sp.dma_start(par[:, :], params).then_inc(param_landed, 16)
            for n, (name, width) in enumerate(CHUNKS):
                if n >= NSLOT:
                    before = CHUNKS[n - NSLOT][0]
                    if before[0] in ("down0", "down1") and before not in LAST_USE:
                        sp.wait_ge(down_read, 5 * int(before[0][-1]) + before[1] + 1)
                    else:
                        sp.wait_ge(bank_filled, FILL_NO[last_use(before)] + 1)
                src = stream[CHUNK_AT[n]:CHUNK_AT[n + 1]].rearrange("(p w) -> p w", p=P)
                sp.dma_start(ring[:, n % NSLOT, 0:width], src).then_inc(chunk_landed[n % NSLOT], 16)
            for t in range(NT):
                sp.wait_ge(out_ready, t + 1)
                sp.dma_start(out[P * t:P * t + P, :], xn[:, t, :]).then_inc(out_stored, 16)
            sp.wait_ge(out_stored, 16 * NT)

        @block.gpsimd
        def _(gp):
            gp.dma_start(pos_i[:, :], positions).then_inc(pos_landed, 16)
            gp.dma_start(t5hot, t5const[0:32, :]).then_inc(t5_landed, 16)
            gp.dma_start(t5ln, t5const[32:32 + HEADS2, :]).then_inc(t5_landed, 16)
            gp.dma_start(t5tab, t5_in).then_inc(t5_landed, 16)
            gp.dma_start(row[:, :], rows.to_broadcast([P, NROW])).then_inc(row_landed, 16)
            nc.gpsimd.memset(pause[:, :], 0.0).then_inc(rpb_cleared, 1)
            nc.gpsimd.memset(rpb_pad, 0.0).then_inc(rpb_cleared, 1)
            gp.wait_ge(rpb_cleared, 2)
            rp = rpb_pad.rearrange("h (r c) -> h r c", r=15)
            gp.dma_start(rp[:, :, 48:79], rpb_in).then_inc(rpb_landed, 16)
            gp.wait_ge(rpb_landed, 16)
            for r in range(RPB_ROWS):
                gp.dma_start(rpb_dram[:, r], rp[:, r + 4, :].unsqueeze(1).to_broadcast([HEADS2, GRID, P])
                             ).then_inc(rpb_stored, 16)
            wait_emptied(gp, ("t5",))
            gp.dma_start(t5_dram, t5vec.unsqueeze(1).to_broadcast([HEADS2, P, REL])).then_inc(t5_stored, 16)
            gp.wait_ge(t5_stored, 16)
            gp.dma_start(tab[:, :, :], bass.AP(tensor=t5_dram.tensor, offset=S - P,
                                               ap=[[REL - 1, P], [P * REL, HEADS2], [1, TABW]])).then_inc(taba_landed, 16)
            gp.wait_ge(rpb_stored, 16 * RPB_ROWS)

            groups = SLOTS // 2

            def gather(t, b, r, fresh):
                n = t * groups + b
                if not fresh:
                    gp.wait_ge(rows_used, r * 4 + (n - 3))
                nc.gpsimd.tensor_copy(stage[:, b, :], experts[:, bass.ds(r * 8 + 2 * n, 2)]).then_inc(stage_ready, 1)
                gp.wait_ge(stage_ready, r * 4 + (n + 1))
                nc.gpsimd.tensor_tensor(pause[:, 1:2], pause[:, 0:1], pause[:, 0:1], ALU.add)
                for k in range(2):
                    gp.indirect_dma_start(out=gath[:, 2 * b + k, :], out_offset=None, in_=uv,
                                          in_offset=bass.IndirectOffsetOnAxis(ap=stage[:, b, k:k + 1], axis=0)
                                          ).then_inc(rows_landed[b], 16)

            for t in range(NT):
                gp.wait_ge(selected, t + 1)
                if t == 0:
                    for b in range(4):
                        gather(t, b, 0, True)
                with gp.Fori(1 - t, groups // 4) as r:
                    for b in range(4):
                        gather(t, b, r, False)

            gp.wait_ge(bank_filled, FILL_NO[("attA", "OT", 0, 0)] + 1)
            for qr in range(2):
                for h in range(HEADS2):
                    gp.dma_start(tab[GRID * qr:GRID * qr + GRID, h, :].rearrange("p (r c) -> p r c", r=6),
                                 bass.AP(tensor=rpb_dram.tensor, offset=(h * RPB_ROWS + 1 - qr) * GRID * P + GRID - 1,
                                         ap=[[P - 1, GRID], [GRID * P, 6], [1, GRID]])).then_inc(tabd_landed, 16)
            gp.dma_start(row[:, LATE["final2"][0]:LATE["final2"][1]],
                         late_rows[:, 0:D].to_broadcast([P, D])).then_inc(late_landed, 16)
            gp.dma_start(row[:, LATE["v_gain"][0]:LATE["v_gain"][1]],
                         late_rows[:, D:D + CW].to_broadcast([P, CW])).then_inc(late_landed, 16)
            gp.wait_ge(tabd_landed, 16 * 2 * HEADS2)
            blocks = tab[:, :, :].rearrange("p h (r c) -> p (h r) c", c=GRID)
            nc.gpsimd.tensor_tensor(blocks, blocks, c_("namask").unsqueeze(1).to_broadcast([P, 6 * HEADS2, GRID]),
                                    ALU.add).then_inc(tabd_ready, 1)

        @block.tensor
        def _(pe):
            filled_so_far = [0]

            def begin(name):
                n = FILL_NO[name]
                assert n == filled_so_far[0], (name, FILLS[filled_so_far[0]])
                filled_so_far[0] += 1
                if n >= RB:
                    pe.wait_ge(bank_emptied[n % RB], n // RB)
                return bank(name)

            def accumulate(dst, pairs):
                for i, (lhsT, rhs) in enumerate(pairs):
                    last = nc.tensor.matmul(dst, lhsT, rhs, start=(i == 0), stop=(i == len(pairs) - 1))
                return last

            def feature_major(name, chunks, act=None):
                act = hT if act is None else act
                for i in range(chunks):
                    w = wait_chunk(pe, (name, i))[:, 0:4096].rearrange("p (k n) -> p k n", k=KD)
                    for pair in range(2):
                        dst = begin((name, i, pair))
                        for j in range(2):
                            c = P * (2 * pair + j)
                            last = accumulate(dst[:, S * j:S * j + S],
                                              [(w[:, k, c:c + P], act[:, k, :]) for k in range(KD)])
                        last.then_inc(bank_filled, 1)

            def token_major(name, i, w, act, kd, n):
                for t in range(NT):
                    dst = begin((name, i, t))
                    accumulate(dst[:, 0:n], [(act[:, k, tile128(t)], w[:, k, :]) for k in range(kd)]
                               ).then_inc(bank_filled, 1)

            def token_major_chunks(name, chunks, act, n=512):
                for i in range(chunks):
                    w = wait_chunk(pe, (name, i))[:, 0:KD * n].rearrange("p (k n) -> p k n", k=KD)
                    token_major(name, i, w, act, KD, n)

            def transposes(name, sources, rows_out=P):
                dst = begin(name)
                for j, src in enumerate(sources):
                    last = nc.tensor.transpose(dst[0:rows_out, P * j:P * j + P], src, ident)
                last.then_inc(bank_filled, 1)

            def norm_transposes(name, src):
                for t in range(NT):
                    pe.wait_ge(xn_ready, xn_before[name] + t + 1)
                    for hf in range(2):
                        transposes((name, t, hf), [src[:, t, P * k:P * k + P] for k in range(4 * hf, 4 * hf + 4)])
                for t in range(NT):
                    for hf in range(2):
                        wait_emptied(pe, (name, t, hf))

            def attention(a):
                def scores_of(h):
                    dst = begin((a.name, "S", h))
                    for t in range(NT):
                        last = nc.tensor.matmul(dst[:, S * t:S * t + S], a.q(h, t), a.k(h), start=True, stop=True)
                    last.then_inc(bank_filled, 1)

                def turn(h):
                    wait_probs(pe, a, h)
                    transposes((a.name, "T", h), [pr_sb[:, h % 2, S * t + P * kt:S * t + P * kt + P]
                                                  for kt in range(NT) for t in range(NT)])

                def values(h):
                    g = first_group[a.name] + h // 8
                    if h % 8 == 0 and g > 0:
                        pe.wait_ge(o_emptied, NT * g)
                    wait_emptied(pe, (a.name, "T", h))
                    c = HD * (h % 8)
                    for t in range(NT):
                        last = accumulate(psum[:, RB + t, c:c + HD],
                                          [(pt_sb[:, h % 2, S * kt + P * t:S * kt + P * t + P], a.v(h, kt))
                                           for kt in range(NT)])
                    last.then_inc(pv_done, 1)

                scores_of(0)
                scores_of(1)
                for h in range(a.heads):
                    turn(h)
                    if h + 2 < a.heads:
                        scores_of(h + 2)
                    if h:
                        values(h - 1)
                values(a.heads - 1)
                for g in range(a.heads // 8):
                    for t in range(NT):
                        pe.wait_ge(o_emptied, NT * (first_group[a.name] + g) + t + 1)
                        c = a.column(g)
                        transposes((a.name, "OT", g, t), [otm[:, t, c + P * j:c + P * j + P] for j in range(4)])

            def wait_turned(a):
                for g in range(a.heads // 8):
                    for t in range(NT):
                        wait_emptied(pe, (a.name, "OT", g, t))

            pe.wait_ge(t5_landed, 48)
            nc.tensor.matmul(begin(("t5",))[0:HEADS2, :], t5tab, t5hot, start=True, stop=True).then_inc(bank_filled, 1)

            pe.wait_ge(const_landed, 16)
            norm_transposes("N1", xn)
            feature_major("glu", 4)
            token_major_chunks("q1", 2, hT)
            token_major_chunks("kv1", 1, hT, 256)
            feature_major("gate", 4)
            pe.wait_ge(conv_ready, 4)
            accumulate(begin(("mean",))[:, 0:S], [(ones, y[:, k, :]) for k in range(KD)]).then_inc(bank_filled, 1)
            pe.wait_ge(ysq_ready, 1)
            accumulate(begin(("var",))[:, 0:S], [(ones, ysq[:, k, :]) for k in range(KD)]).then_inc(bank_filled, 1)
            for t in range(NT):
                pe.wait_ge(rope_ready, t + 1)
                for hf in range(2):
                    transposes(("q1T", t, hf), [qkr[:, t, P * k:P * k + P] for k in range(4 * hf, 4 * hf + 4)])
            transposes(("k1T",), [kdup[:, t, n].rearrange("p c d -> p (c d)") for n in range(KVH) for t in range(NT)])
            for t in range(NT):
                for hf in range(2):
                    wait_emptied(pe, ("q1T", t, hf))
                wait_emptied(pe, ("kv1", 0, t))
            wait_emptied(pe, ("k1T",))
            attention(att1)
            pe.wait_ge(silu_ready, 1)
            feature_major("convout", 2, y)
            wait_turned(att1)
            feature_major("attno", 2, oT)
            pe.wait_ge(merged_ready, 1)
            token_major_chunks("wout", 2, hT)
            norm_transposes("N2", xn)
            feature_major("pq", 4)
            for i in range(4):
                for pair in range(2):
                    wait_emptied(pe, ("pq", i, pair))
            keys = wait_chunk(pe, ("keys", 0))[:, 0:2048].rearrange("p (m n) -> p m n", n=NKEYS)
            for t in range(NT):
                for j in range(4):
                    dst = begin(("sc", t, j))
                    for m in range(4 * j, 4 * j + 4):
                        c = NKEYS * (m - 4 * j)
                        last = nc.tensor.matmul(dst[:, c:c + NKEYS], qpT[:, m, tile128(t)], keys[:, m, :],
                                                start=True, stop=True)
                    last.then_inc(bank_filled, 1)

            norm_transposes("mix0", xn)
            feature_major("qa", 1)
            feature_major("ka", 1)
            token_major_chunks("va", 1, hT)
            token_major_chunks("cqkv", 2, hT)
            for name in ("qa", "ka"):
                for pair in range(2):
                    wait_emptied(pe, (name, 0, pair))
            for t in range(NT):
                wait_emptied(pe, ("va", 0, t))
            attention(attA)
            norm_transposes("cT", cqkv)
            w = wait_chunk(pe, ("kpe_uq", 0))
            token_major("kpe", 0, w[:, 0:256].rearrange("p (k n) -> p k n", k=KD), hT, KD, ROPE2)
            token_major("uqa", 0, w[:, 256:3328].rearrange("p (k n) -> p k n", k=6), cT, 6, 512)
            w = wait_chunk(pe, ("uq_ukv", 0))
            token_major("uqb", 0, w[:, 0:1536].rearrange("p (k n) -> p k n", k=6), cT, 6, 256)
            for i in range(2):
                token_major("ukv", i, w[:, 1536:3584].rearrange("p (k n) -> p k n", k=2)[:, :, 512 * i:512 * i + 512],
                            cT[:, 6:8, :], 2, 512)
            for n, src in (("qmT", uq), ("kmT", km)):
                for t in range(NT):
                    pe.wait_ge(rope_ready, NT + t + 1)
                    for hf in range(2):
                        transposes((n, t, hf), [src[:, t, QK2 * h:QK2 * h + QK2] for h in range(4 * hf, 4 * hf + 4)],
                                   QK2)
            for n in ("qmT", "kmT"):
                for t in range(NT):
                    for hf in range(2):
                        wait_emptied(pe, (n, t, hf))
            for i in range(2):
                for t in range(NT):
                    wait_emptied(pe, ("ukv", i, t))
            attention(attB)
            wait_turned(attA)
            wait_turned(attB)
            token_major_chunks("evout", 2, oT)

            def feed_forward(layer):
                norm_transposes("ffn%d" % layer, xn)
                feature_major("gu%d" % layer, KF // 2)
                name = "down%d" % layer
                banks = {(n, t): begin((name, n, t)) for n in range(2) for t in range(NT)}
                for k in range(KF):
                    if k % 4 == 0:
                        w = wait_chunk(pe, (name, k // 4))
                    if k % 2 == 0:
                        wait_emptied(pe, ("gu%d" % layer, k // 2, 1))
                    for n in range(2):
                        for t in range(NT):
                            c = D * (k % 4) + 512 * n
                            last = nc.tensor.matmul(banks[n, t], guT[:, k, tile128(t)], w[:, c:c + 512],
                                                    start=(k == 0), stop=(k == KF - 1))
                            if k == KF - 1:
                                last.then_inc(bank_filled, 1)
                    if k % 4 == 3:
                        last.then_inc(down_read, 1)

            feed_forward(0)
            norm_transposes("mix1", xn)
            token_major_chunks("uz", 1, hT)
            token_major_chunks("vz", 1, hT)
            feature_major("qd", 1)
            feature_major("kd", 1)
            token_major_chunks("vd", 1, hT)
            ws = wait_chunk(pe, ("ws", 0))[:, 0:1024].rearrange("p (g i) -> p g i", g=8)
            for t in range(NT):
                pe.wait_ge(vn_ready, t + 1)
                dst = begin(("gating", t))
                for g in range(8):
                    last = nc.tensor.matmul(dst[:, 64 * g:64 * g + 64], ws[:, g, :], vz[:, t, 64 * g:64 * g + 64],
                                            start=True, stop=True)
                last.then_inc(bank_filled, 1)
            for t in range(NT):
                pe.wait_ge(cout_ready, t + 1)
                transposes(("coutT", t), [cout[:, t, P * j:P * j + P] for j in range(4)])
            for name in ("qd", "kd"):
                for pair in range(2):
                    wait_emptied(pe, (name, 0, pair))
            for t in range(NT):
                wait_emptied(pe, ("vd", 0, t))
            attention(attD)
            for t in range(NT):
                wait_emptied(pe, ("coutT", t))
            wait_turned(attD)
            token_major_chunks("odout", 2, oT)
            feed_forward(1)
            assert filled_so_far[0] == len(FILLS)

        @block.scalar
        def _(act):
            steps = [0]

            def step(ins):
                steps[0] += 1
                ins.then_inc(scalar_step, 1)
                act.wait_ge(scalar_step, steps[0])

            def empty(name, dst, src=None, func=ACT.Copy):
                b = wait_filled(act, name)
                nc.scalar.activation(dst, b if src is None else src(b), func).then_inc(emptied_sem(name), 1)

            def root(src, junk, total, column, width):
                step(nc.scalar.activation(junk, src, ACT.Square, accum_out=total))
                nc.scalar.activation(rstd[:, column:column + 1], total, ACT.Sqrt, bias=eps,
                                     scale=1.0 / width).then_inc(root_ready, 1)

            def norm_roots(after):
                for t in range(NT):
                    for name in (after(t) if after else ()):
                        wait_emptied(act, name)
                    root(x[:, t, :], xn[:, t, :], ssq[:, t:t + 1], t, D)

            def sums(name):
                return lambda t: [(name, i, t) for i in range(2)]

            def copies(name, t_or_pair, dst):
                for j in range(2):
                    empty((name, t_or_pair, j), dst(j))

            def attention(a):
                def exponentials(h):
                    n = first_head[a.name] + h
                    if h >= 2:
                        act.wait_ge(bank_filled, FILL_NO[(a.name, "T", h - 2)] + 1)
                    act.wait_ge(nmax_ready, n + 1)
                    src = bank((a.name, "S", h)) if a.table is None else sc_sb[:, h % 2, :]
                    for t in range(NT):
                        last = nc.scalar.activation(pr_sb[:, h % 2, S * t:S * t + S], src[:, S * t:S * t + S], ACT.Exp,
                                                    bias=nmax[:, h, t:t + 1], scale=a.scale if a.table is None else 1.0,
                                                    accum_out=den[:, h, t:t + 1])
                    last.then_inc(emptied_sem((a.name, "S", h)) if a.table is None else probs_ready, 1)

                def turned(h):
                    if h >= 2:
                        act.wait_ge(pv_done, first_head[a.name] + h - 1)
                    empty((a.name, "T", h), pt_sb[:, h % 2, :])

                for h in range(a.heads):
                    exponentials(h)
                    if a.sinks and h % 8 == 7:
                        act.wait_ge(nmaxs_ready, h // 8 + 1)
                        w = sinkw[:, h - 7:h + 1, :]
                        nc.scalar.activation(w, w, ACT.Exp).then_inc(sinkw_ready, 1)
                    if h:
                        turned(h - 1)
                turned(a.heads - 1)
                for g in range(a.heads // 8):
                    for t in range(NT):
                        c = a.column(g) // P
                        empty((a.name, "OT", g, t), oT[:, c:c + 4, tile128(t)],
                              lambda b: b.rearrange("p (k n) -> p k n", k=4))

            act.wait_ge(x_landed, 16)
            act.wait_ge(eps_ready, 1)
            norm_roots(None)
            act.wait_ge(param_landed, 16)
            for i in range(4):
                if i >= 2:
                    wait_emptied(act, ("glu", i - 2, 0))
                b = wait_filled(act, ("glu", i, 1))
                for j in range(2):
                    m = 8 + 2 * i + j
                    last = nc.scalar.activation(glu_sig[:, i % 2, S * j:S * j + S], b[:, S * j:S * j + S], ACT.Sigmoid,
                                                bias=par_("b_glu")[:, m:m + 1])
                last.then_inc(emptied_sem(("glu", i, 1)), 1)
            for i in range(4):
                for pair in range(2):
                    b = wait_filled(act, ("gate", i, pair))
                    for j in range(2):
                        m = 4 * i + 2 * pair + j
                        dst = (sgc if m < KD else sga)[:, m % KD, :]
                        last = nc.scalar.activation(dst, b[:, S * j:S * j + S], ACT.Sigmoid,
                                                    bias=par_("b_gate")[:, m:m + 1])
                    last.then_inc(emptied_sem(("gate", i, pair)), 1)
            act.wait_ge(angle_ready, 1)
            nc.scalar.activation(angles[:, 2:4, :, :], angles[:, 0:2, :, :], ACT.Sin).then_inc(trig_ready, 1)
            wait_emptied(act, ("mean",))
            nc.scalar.activation(ysq, y, ACT.Square).then_inc(ysq_ready, 1)
            b = wait_filled(act, ("var",))
            nc.scalar.activation(sc_sb[:, 0, 0:S], b[:, 0:S], ACT.Sqrt, bias=eps,
                                 scale=1.0 / D).then_inc(emptied_sem(("var",)), 1)
            act.wait_ge(ynorm_ready, 1)
            for m in range(KD):
                last = nc.scalar.activation(y[:, m, :], y[:, m, :], ACT.Silu, bias=par_("ln_b")[:, m:m + 1],
                                            scale=par_("ln_g")[:, m:m + 1])
            last.then_inc(silu_ready, 1)
            for t in range(NT):
                for hf in range(2):
                    empty(("q1T", t, hf), q1T[:, 4 * hf:4 * hf + 4, tile128(t)],
                          lambda b: b.rearrange("p (k n) -> p k n", k=4))
            empty(("k1T",), k1T.rearrange("p n s -> p (n s)"))
            attention(att1)
            norm_roots(sums("wout"))
            for i in range(4):
                for pair in range(2):
                    m = 4 * i + 2 * pair
                    empty(("pq", i, pair), qpT[:, m:m + 2, :].rearrange("p a b -> p (a b)"))
            for t in range(NT):
                for j in range(4):
                    empty(("sc", t, j), scores[:, t, 512 * j:512 * j + 512])
            for t in range(NT):
                act.wait_ge(shifted_ready, t + 1)
                g = gates[:, SLOTS * t:SLOTS * t + SLOTS]
                nc.scalar.activation(g, g, ACT.Exp).then_inc(best_exp_ready, 1)
            with act.Fori(0, NT * SLOTS // 8) as r:
                for b in range(4):
                    act.wait_ge(dots_ready, r * 4 + (b + 1))
                    nc.scalar.activation(acts[:, b, :], dots[:, b, :], ACT.Gelu).then_inc(acts_ready, 1)
            for t in range(NT):
                act.wait_ge(rows_used, SLOTS // 2 * (t + 1))
                root(x[:, t, :], xn[:, t, :], ssq[:, t:t + 1], t, D)
            for t in range(NT):
                act.wait_ge(x_normed, t + 1)
                root(x[:, t, :], xn[:, t, :], ssq[:, t:t + 1], t, D)
            for name, dst in (("qa", qaT), ("ka", kaT)):
                for pair in range(2):
                    empty((name, 0, pair), dst[:, 2 * pair:2 * pair + 2, :].rearrange("p a b -> p (a b)"))
            for t in range(NT):
                empty(("va", 0, t), va[:, t, :])
            for i in range(2):
                for t in range(NT):
                    empty(("cqkv", i, t), cqkv[:, t, 512 * i:512 * i + 512])
            for t in range(NT):
                for i, (lo, hi) in enumerate(((0, QRANK), (QRANK, D))):
                    wait_emptied(act, ("cqkv", 1, t))
                    root(cqkv[:, t, lo:hi], xn[:, t, lo:hi], ssq[:, i:i + 1], 2 * i + t, hi - lo)
            attention(attA)
            for t in range(NT):
                empty(("kpe", 0, t), kpe[:, t, :], lambda b: b[:, 0:ROPE2])
            for t in range(NT):
                empty(("uqa", 0, t), uq[:, t, 0:512])
            for t in range(NT):
                empty(("uqb", 0, t), uq[:, t, 512:QRANK], lambda b: b[:, 0:256])
            for i in range(2):
                for t in range(NT):
                    empty(("ukv", i, t), ukv[:, t, 512 * i:512 * i + 512])
            for n, dst in (("qmT", qmT), ("kmT", kmT)):
                for t in range(NT):
                    for hf in range(2):
                        empty((n, t, hf), dst[0:QK2, 4 * hf:4 * hf + 4, tile128(t)],
                              lambda b: b[0:QK2, :].rearrange("p (k n) -> p k n", k=4))
            attention(attB)
            norm_roots(sums("evout"))

            def feed_forward(layer):
                name = "gu%d" % layer
                for i in range(KF // 2):
                    if i >= 2:
                        wait_emptied(act, (name, i - 2, 1))
                    b = wait_filled(act, (name, i, 0))
                    nc.scalar.activation(silu[:, i % 2, :], b, ACT.Silu).then_inc(emptied_sem((name, i, 0)), 1)

            feed_forward(0)
            norm_roots(lambda t: [("down0", n, t) for n in range(2)])
            for name, dst in (("uz", uz), ("vz", vz)):
                for t in range(NT):
                    empty((name, 0, t), dst[:, t, :], func=ACT.Gelu_apprx_tanh)
            for t in range(NT):
                act.wait_ge(vcen_ready, t + 1)
                step(nc.scalar.activation(xn[:, t, 0:CW], vz[:, t, :], ACT.Square, accum_out=ssq[:, t:t + 1]))
                nc.scalar.activation(rstd[:, t:t + 1], ssq[:, t:t + 1], ACT.Sqrt, bias=eps,
                                     scale=1.0 / CW).then_inc(vroot_ready, 1)
            for name, dst in (("qd", qdT), ("kd", kdT)):
                for pair in range(2):
                    empty((name, 0, pair), dst[:, 2 * pair:2 * pair + 2, :].rearrange("p a b -> p (a b)"))
            for t in range(NT):
                empty(("vd", 0, t), vd[:, t, :])
            for t in range(NT):
                empty(("coutT", t), oT[:, 0:4, tile128(t)], lambda b: b.rearrange("p (k n) -> p k n", k=4))
            attention(attD)
            norm_roots(sums("odout"))
            feed_forward(1)
            norm_roots(lambda t: [("down1", n, t) for n in range(2)])

        @block.vector
        def _(dve):
            steps = [0]

            def mark(ins):
                steps[0] += 1
                ins.then_inc(vector_step, 1)
                return steps[0]

            def after(n):
                dve.wait_ge(vector_step, n)

            def link(ins):
                after(mark(ins))

            V = nc.vector

            def normed(name, src=None, dst=None, rows_=None, signal=None):
                for t in range(NT):
                    dve.wait_ge(root_ready, roots_before[name] + t + 1)
                    r = rstd[:, t:t + 1]
                    link(V.reciprocal(r, r))
                    d = (xn if dst is None else dst)[:, t, :]
                    if rows_ is None:
                        ins = V.tensor_scalar(d, x[:, t, :], r, None, ALU.mult)
                    else:
                        ins = V.scalar_tensor_tensor(d, x[:, t, :], r, rows_, ALU.mult, ALU.mult)
                    ins.then_inc(xn_ready if signal is None else signal, 1)

            def gained(name, dst):
                g = par_(gain_of[name]) if name in gain_of else None
                for t in range(NT):
                    for hf in range(2):
                        b = wait_filled(dve, (name, t, hf)).rearrange("p (k n) -> p k n", k=4)
                        d = dst[:, 4 * hf:4 * hf + 4, tile128(t)]
                        if g is None:
                            ins = V.tensor_copy(d, b)
                        else:
                            ins = V.tensor_tensor(d, b, g[:, 4 * hf:4 * hf + 4].unsqueeze(2).to_broadcast([P, 4, P]),
                                                  ALU.mult)
                        ins.then_inc(emptied_sem((name, t, hf)), 1)

            def add_to_x(name):
                for i in range(2):
                    for t in range(NT):
                        b = wait_filled(dve, (name, i, t))
                        d = x[:, t, 512 * i:512 * i + 512]
                        V.tensor_tensor(d, d, b, ALU.add).then_inc(emptied_sem((name, i, t)), 1)

            def attention(a):
                def divide(g):
                    dg = den[:, 8 * g:8 * g + 8, :]
                    wait_probs(dve, a, 8 * g + 7)
                    if a.sinks:
                        dve.wait_ge(sinkw_ready, g + 1)
                        link(V.tensor_tensor(dg, dg, sinkw[:, 8 * g:8 * g + 8, :], ALU.add))
                    link(V.reciprocal(dg, dg))
                    dve.wait_ge(pv_done, first_head[a.name] + 8 * g + 8)
                    for t in range(NT):
                        c = a.column(g)
                        V.tensor_tensor(otm[:, t, c:c + 512].rearrange("p (h d) -> p h d", h=8),
                                        psum[:, RB + t, :].rearrange("p (h d) -> p h d", h=8),
                                        dg[:, :, t].unsqueeze(2).to_broadcast([P, 8, HD]),
                                        ALU.mult).then_inc(o_emptied, 1)

                for h in range(a.heads):
                    n = first_head[a.name] + h
                    b = wait_filled(dve, (a.name, "S", h))
                    if a.table is not None:
                        if h >= 2:
                            wait_probs(dve, a, h - 2)
                        for t in range(NT):
                            ins = V.scalar_tensor_tensor(sc_sb[:, h % 2, S * t:S * t + S], b[:, S * t:S * t + S],
                                                         a.scale, a.table(h)[:, P - P * t:P - P * t + S],
                                                         ALU.mult, ALU.add)
                        ins.then_inc(emptied_sem((a.name, "S", h)), 1)
                        wait_emptied(dve, (a.name, "S", h))
                        src = sc_sb[:, h % 2, :]
                    else:
                        src = b
                    m = nmax[:, h, :]
                    ins = V.tensor_reduce(m, src.rearrange("p (t k) -> p t k", t=NT), AX, ALU.max, negate=True)
                    if a.table is None:
                        link(ins)
                        ins = V.tensor_scalar(m, m, a.scale, None, ALU.mult)
                    if a.sinks:
                        link(ins)
                        ins = V.tensor_scalar(m, m, nsink[:, h:h + 1], None, ALU.min)
                    ins.then_inc(nmax_ready, 1)
                    if a.sinks and h % 8 == 7:
                        dve.wait_ge(nmax_ready, n + 1)
                        V.tensor_tensor(sinkw[:, h - 7:h + 1, :], nmax[:, h - 7:h + 1, :],
                                        nsink[:, h - 7:h + 1].unsqueeze(2).to_broadcast([P, 8, NT]),
                                        ALU.subtract).then_inc(nmaxs_ready, 1)
                    if h == 8:
                        divide(0)
                divide(a.heads // 8 - 1)

            V.memset(eps, EPS).then_inc(eps_ready, 1)
            link(V.memset(u[:, :, 0:TAPS - 1], 0.0))
            b = wait_filled(dve, ("t5",))
            V.tensor_tensor(t5vec, b[0:HEADS2, :], t5ln, ALU.add).then_inc(emptied_sem(("t5",)), 1)

            normed("N1")
            dve.wait_ge(param_landed, 16)
            gained("N1", hT)

            def conv_pair(i):
                for w in range(TAPS):
                    for m in (2 * i, 2 * i + 1):
                        src, tap = u[:, m, w:w + S], conv_w[:, m, w:w + 1]
                        if w == 0:
                            n = mark(V.tensor_scalar(y[:, m, :], src, tap, par_("conv_b")[:, m:m + 1],
                                                     ALU.mult, ALU.add))
                        elif w == TAPS - 1 and m == 2 * i + 1:
                            after(steps[0] - 1)
                            V.scalar_tensor_tensor(y[:, m, :], src, tap, y[:, m, :], ALU.mult, ALU.add
                                                   ).then_inc(conv_ready, 1)
                        else:
                            after(steps[0] - 1)
                            n = mark(V.scalar_tensor_tensor(y[:, m, :], src, tap, y[:, m, :], ALU.mult, ALU.add))
                return n

            for i in range(4):
                wait_emptied(dve, ("glu", i, 1))
                b = wait_filled(dve, ("glu", i, 0))
                for j in range(2):
                    m = 2 * i + j
                    ins = V.scalar_tensor_tensor(u[:, m, TAPS - 1:], b[:, S * j:S * j + S], par_("b_glu")[:, m:m + 1],
                                                 glu_sig[:, i % 2, S * j:S * j + S], ALU.add, ALU.mult)
                ins.then_inc(emptied_sem(("glu", i, 0)), 1)
                if i:
                    conv_pair(i - 1)
                wait_emptied(dve, ("glu", i, 0))
            dve.wait_ge(row_landed, 16)
            for i in range(2):
                for t in range(NT):
                    b = wait_filled(dve, ("q1", i, t))
                    V.tensor_tensor(qkv[:, t, 512 * i:512 * i + 512], b, row_("b_qkv")[:, 512 * i:512 * i + 512],
                                    ALU.add).then_inc(emptied_sem(("q1", i, t)), 1)
            for t in range(NT):
                b = wait_filled(dve, ("kv1", 0, t))
                V.tensor_tensor(qkv[:, t, 1024:1280], b[:, 0:256], row_("b_qkv")[:, 1024:1280],
                                ALU.add).then_inc(emptied_sem(("kv1", 0, t)), 1)
            conv_pair(3)
            dve.wait_ge(pos_landed, 16)
            dve.wait_ge(const_landed, 16)
            link(V.tensor_copy(posf, pos_i[:, :]))
            raw, turns = angles[:, 0, :, :], angles[:, 1, :, :]
            for t in range(NT):
                n = mark(V.tensor_scalar(angles[:, 0, t, :], c_("inv"), posf[:, t:t + 1], None, ALU.mult))
            after(n)
            link(V.tensor_scalar(turns, raw, float(1 / (2 * np.pi)), None, ALU.mult))
            link(V.tensor_scalar(turns, turns, 12582912.0, None, ALU.add))
            link(V.tensor_scalar(turns, turns, -12582912.0, None, ALU.add))
            c1 = 6.28125
            c2 = float(np.float32(2 * np.pi - c1)) - float(np.float32(2 * np.pi - c1)) % 2.0 ** -20
            c3 = float(2 * np.pi - c1 - c2)
            for c in (c1, c2, c3):
                link(V.scalar_tensor_tensor(raw, turns, -c, raw, ALU.mult, ALU.add))
            lim = float(np.nextafter(np.float32(np.pi), np.float32(0)))
            link(V.tensor_scalar(raw, raw, lim, -lim, ALU.min, ALU.max))
            link(V.scalar_tensor_tensor(turns, raw, -1.0, raw, ALU.mult, ALU.min))
            V.tensor_scalar(turns, turns, float(np.pi / 2), None, ALU.add).then_inc(angle_ready, 1)
            b = wait_filled(dve, ("mean",))
            V.scalar_tensor_tensor(y, b[:, 0:S].unsqueeze(1).to_broadcast([P, KD, S]), -1.0 / D, y,
                                   ALU.mult, ALU.add).then_inc(emptied_sem(("mean",)), 1)
            dve.wait_ge(trig_ready, 1)
            dve.wait_ge(t5_stored, 16)
            dve.wait_ge(rpb_stored, 16 * RPB_ROWS)
            for t in range(NT):
                wait_emptied(dve, ("q1", 0, t))
                wait_emptied(dve, ("q1", 1, t))
                wait_emptied(dve, ("kv1", 0, t))
                heads = qkv[:, t, 0:18 * HD].rearrange("p (h d) -> p h d", d=HD)
                turned = qkr[:, t, :].rearrange("p (h d) -> p h d", d=HD)
                sin = angles[:, 2, t, :].unsqueeze(1).to_broadcast([P, 18, 32])
                cos = angles[:, 3, t, :].unsqueeze(1).to_broadcast([P, 18, 32])
                lo, hi = heads[:, :, 0:32], heads[:, :, 32:64]
                V.tensor_tensor(rope_tmp[:, 0], lo, cos, ALU.mult)
                V.tensor_tensor(rope_tmp[:, 1], hi, sin, ALU.mult)
                V.tensor_tensor(rope_tmp[:, 2], hi, cos, ALU.mult)
                link(V.tensor_tensor(rope_tmp[:, 3], lo, sin, ALU.mult))
                V.tensor_tensor(turned[:, :, 0:32], rope_tmp[:, 0], rope_tmp[:, 1], ALU.subtract)
                link(V.tensor_tensor(turned[:, :, 32:64], rope_tmp[:, 2], rope_tmp[:, 3], ALU.add))
                for c in range(2):
                    ins = V.tensor_copy(kdup[:, t, :, c, :], turned[:, 16:18, :])
                ins.then_inc(rope_ready, 1)
            wait_emptied(dve, ("var",))
            dev = sc_sb[:, 0, 0:S]
            link(V.reciprocal(dev, dev))
            V.tensor_tensor(y, y, dev.unsqueeze(1).to_broadcast([P, KD, S]), ALU.mult).then_inc(ynorm_ready, 1)
            link(V.tensor_scalar(nsink, row_("sinks"), -1.0, None, ALU.mult))
            dve.wait_ge(ynorm_ready, 1)
            attention(att1)
            for name, g in (("convout", sgc), ("attno", sga)):
                for i in range(2):
                    for pair in range(2):
                        b = wait_filled(dve, (name, i, pair))
                        m = 4 * i + 2 * pair
                        wait_emptied(dve, ("gate", i + (2 if name == "attno" else 0), pair))
                        d = g[:, m:m + 2, :].rearrange("p a b -> p (a b)")
                        V.tensor_tensor(d, d, b, ALU.mult).then_inc(emptied_sem((name, i, pair)), 1)
            for name in ("convout", "attno"):
                for i in range(2):
                    for pair in range(2):
                        wait_emptied(dve, (name, i, pair))
            V.tensor_tensor(hT[:, :, :], sgc, sga, ALU.add).then_inc(merged_ready, 1)
            add_to_x("wout")
            normed("N2", rows_=row_("norm2"))
            gained("N2", hT)

            def top16(src, values, indices):
                link(V.max(values[:, 0:8], src))
                V.max_index(indices[:, 0:8], values[:, 0:8], src)
                link(V.match_replace(src, values[:, 0:8], src, -3.0e38))
                link(V.max(values[:, 8:16], src))
                link(V.max_index(indices[:, 8:16], values[:, 8:16], src))

            for t in range(NT):
                for j in range(4):
                    wait_emptied(dve, ("sc", t, j))
                for m in range(2 * PH):
                    top16(scores[:, t, NKEYS * m:NKEYS * m + NKEYS], topv[:, m, :], topi[:, m, :])
                link(V.tensor_copy(topf[:, :, :], topi[:, :, :]))
                tv = topv[:, :, :].rearrange("p (h c) k -> p h c k", c=2)
                tf = topf[:, :, :].rearrange("p (h c) k -> p h c k", c=2)
                shape = [P, PH, TOPK, TOPK]
                grid = cand.rearrange("p h (i j) -> p h i j", i=TOPK)
                link(V.tensor_tensor(grid, tv[:, :, 0, :].unsqueeze(3).to_broadcast(shape),
                                     tv[:, :, 1, :].unsqueeze(2).to_broadcast(shape), ALU.add))
                for h in range(PH):
                    top16(cand[:, h, :], best[:, h, :], bpos[:, h, :])
                g = gates[:, SLOTS * t:SLOTS * t + SLOTS].rearrange("p (h k) -> p h k", h=PH)
                V.tensor_tensor(g, best[:, :, :], best[:, :, 0:1].to_broadcast([P, PH, TOPK]), ALU.subtract
                                ).then_inc(shifted_ready, 1)
                V.tensor_scalar(bdig[:, 0], bpos[:, :, :], 4, None, ALU.logical_shift_right)
                link(V.tensor_scalar(bdig[:, 1], bpos[:, :, :], 15, None, ALU.bitwise_and))
                link(V.tensor_copy(bdigf[:, :, :, :], bdig[:, :, :, :]))
                iota = c_("iota").unsqueeze(1).unsqueeze(1).to_broadcast(shape)
                for c in range(2):
                    link(V.tensor_tensor(grid, bdigf[:, c].unsqueeze(3).to_broadcast(shape), iota, ALU.is_equal))
                    link(V.tensor_tensor(grid, grid, tf[:, :, c, :].unsqueeze(2).to_broadcast(shape), ALU.mult))
                    link(V.tensor_reduce(hits[:, c], grid, AX, ALU.add))
                dve.wait_ge(best_exp_ready, t + 1)
                link(V.tensor_reduce(gsum[:, :], g, AX, ALU.add))
                link(V.reciprocal(gsum[:, :], gsum[:, :]))
                link(V.tensor_tensor(g, g, gsum[:, :].unsqueeze(2).to_broadcast([P, PH, TOPK]), ALU.mult))
                V.scalar_tensor_tensor(experts[:, SLOTS * t:SLOTS * t + SLOTS], hits[:, 0].rearrange("p h k -> p (h k)"),
                                       float(NKEYS), hits[:, 1].rearrange("p h k -> p (h k)"), ALU.mult, ALU.add
                                       ).then_inc(selected, 1)

            groups = SLOTS // 2
            base = steps[0]

            def dot(t, b, r, shift, k):
                n = t * groups + shift
                if k == 0:
                    dve.wait_ge(rows_landed[b], r * 32 + 32 * (n // 4 + 1))
                row_u = gath[:, 2 * b + k, 0:D]
                ins = V.tensor_tensor_reduce(out=row_u, in0=row_u, in1=xn[:, t, :], scale=1.0,
                                             scalar=0.0, op0=ALU.mult, op1=ALU.add, accum_out=dots[:, b, k:k + 1])
                if k == 1:
                    ins.then_inc(dots_ready, 1)

            def weigh(t, b, r, shift):
                n = t * groups + shift
                dve.wait_ge(acts_ready, r * 4 + (n + 1))
                V.tensor_tensor(coef[:, b, :], acts[:, b, :], gates[:, bass.ds(r * 8 + 2 * n, 2)], ALU.mult
                                ).then_inc(vector_step, 1)
                dve.wait_ge(vector_step, r * 8 + (base + 2 * n + 1))

            def add_row(t, b, r, shift, k):
                n = t * groups + shift
                ins = V.scalar_tensor_tensor(x[:, t, :], gath[:, 2 * b + k, D:2 * D], coef[:, b, k:k + 1], x[:, t, :],
                                             ALU.mult, ALU.add)
                if k == 0:
                    ins.then_inc(vector_step, 1)
                    dve.wait_ge(vector_step, r * 8 + (base + 2 * n + 2))
                else:
                    ins.then_inc(rows_used, 1)

            def group(t, b, r, ahead):
                if ahead:
                    dot(t, (b + 1) % 4, r, b + 1, 0)
                weigh(t, b, r, b)
                add_row(t, b, r, b, 0)
                if ahead:
                    dot(t, (b + 1) % 4, r, b + 1, 1)
                add_row(t, b, r, b, 1)
                dve.wait_ge(rows_used, r * 4 + (t * groups + b + 1))

            for t in range(NT):
                dot(t, 0, 0, 0, 0)
                dot(t, 0, 0, 0, 1)
                with dve.Fori(0, groups // 4 - 1) as r:
                    for b in range(4):
                        group(t, b, r, True)
                for b in range(4):
                    group(t, b, groups // 4 - 1, b < 3)
            steps[0] = base + 2 * NT * groups

            dve.wait_ge(rows_used, NT * groups)
            normed("F1", dst=x, rows_=row_("final1"), signal=x_normed)
            normed("mix0")
            gained("mix0", hT)
            for t in range(NT):
                for i, (lo, hi) in enumerate(((0, QRANK), (QRANK, D))):
                    c = 2 * i + t
                    dve.wait_ge(root_ready, roots_before["cT"] + 2 * t + i + 1)
                    link(V.reciprocal(rstd[:, c:c + 1], rstd[:, c:c + 1]))
                    ins = V.tensor_scalar(cqkv[:, t, lo:hi], cqkv[:, t, lo:hi], rstd[:, c:c + 1], None, ALU.mult)
                ins.then_inc(xn_ready, 1)
            dve.wait_ge(taba_landed, 16)
            attention(attA)
            gained("cT", cT)
            for t in range(NT):
                for name in (("kpe", 0, t), ("uqa", 0, t), ("uqb", 0, t), ("ukv", 0, t), ("ukv", 1, t)):
                    wait_emptied(dve, name)
                cos = c_("cos2")[:, 16 * t:16 * t + 16]
                sin = c_("sin2")[:, 16 * t:16 * t + 16]
                qh = uq[:, t, :].rearrange("p (h d) -> p h d", h=HEADS2)
                kh = km[:, t, :].rearrange("p (h d) -> p h d", h=HEADS2)
                eight = [P, HEADS2, 16]
                tmp = xn[:, t, 0:640].rearrange("p (a h d) -> p a h d", a=5, h=HEADS2)
                lo, hi = qh[:, :, NOPE:NOPE + 16], qh[:, :, NOPE + 16:QK2]
                cb, sb_ = cos.unsqueeze(1).to_broadcast(eight), sin.unsqueeze(1).to_broadcast(eight)
                V.tensor_tensor(tmp[:, 0], lo, cb, ALU.mult)
                V.tensor_tensor(tmp[:, 1], hi, sb_, ALU.mult)
                V.tensor_tensor(tmp[:, 2], lo, sb_, ALU.mult)
                V.tensor_tensor(tmp[:, 3], hi, cb, ALU.mult)
                ktmp = tmp[:, 4]
                klo, khi = kpe[:, t, 0:16], kpe[:, t, 16:32]
                V.tensor_tensor(ktmp[:, 0, :], klo, cos, ALU.mult)
                V.tensor_tensor(ktmp[:, 1, :], khi, sin, ALU.mult)
                V.tensor_tensor(ktmp[:, 2, :], klo, sin, ALU.mult)
                link(V.tensor_tensor(ktmp[:, 3, :], khi, cos, ALU.mult))
                V.tensor_tensor(lo, tmp[:, 0], tmp[:, 1], ALU.subtract)
                V.tensor_tensor(hi, tmp[:, 2], tmp[:, 3], ALU.add)
                V.tensor_tensor(kh[:, :, NOPE:NOPE + 16], ktmp[:, 0:1, :].to_broadcast(eight),
                                ktmp[:, 1:2, :].to_broadcast(eight), ALU.subtract)
                V.tensor_tensor(kh[:, :, NOPE + 16:QK2], ktmp[:, 2:3, :].to_broadcast(eight),
                                ktmp[:, 3:4, :].to_broadcast(eight), ALU.add)
                V.tensor_copy(kh[:, :, 0:NOPE], ukv[:, t, :].rearrange("p (h d) -> p h d", h=HEADS2)[:, :, 0:NOPE]
                              ).then_inc(rope_ready, 1)
            attention(attB)
            add_to_x("evout")

            def feed_forward(layer):
                normed("ffn%d" % layer)
                gained("ffn%d" % layer, hT)
                name = "gu%d" % layer
                for i in range(KF // 2):
                    wait_emptied(dve, (name, i, 0))
                    b = wait_filled(dve, (name, i, 1))
                    V.tensor_tensor(guT[:, 2 * i:2 * i + 2, :].rearrange("p a b -> p (a b)"), silu[:, i % 2, :], b,
                                    ALU.mult).then_inc(emptied_sem((name, i, 1)), 1)
                add_to_x("down%d" % layer)

            feed_forward(0)
            normed("mix1")
            gained("mix1", hT)
            dve.wait_ge(late_landed, 32)
            for t in range(NT):
                wait_emptied(dve, ("vz", 0, t))
                link(V.tensor_reduce(vsum[:, t:t + 1], vz[:, t, :], AX, ALU.add, negate=True))
                link(V.tensor_scalar(vsum[:, t:t + 1], vsum[:, t:t + 1], 1.0 / CW, None, ALU.mult))
                V.tensor_scalar(vz[:, t, :], vz[:, t, :], vsum[:, t:t + 1], None, ALU.add).then_inc(vcen_ready, 1)
            gain = row[:, LATE["v_gain"][0]:LATE["v_gain"][1]]
            for t in range(NT):
                dve.wait_ge(vroot_ready, t + 1)
                dve.wait_ge(vcen_ready, t + 1)
                link(V.reciprocal(rstd[:, t:t + 1], rstd[:, t:t + 1]))
                V.scalar_tensor_tensor(vz[:, t, :], vz[:, t, :], rstd[:, t:t + 1], gain, ALU.mult, ALU.mult
                                       ).then_inc(vn_ready, 1)
            for t in range(NT):
                b = wait_filled(dve, ("gating", t)).rearrange("p (g c) -> p g c", g=8)
                co = cout[:, t, :].rearrange("p (g c) -> p g c", g=8)
                V.tensor_tensor(co, b, par_("b_s").unsqueeze(2).to_broadcast([P, 8, 64]), ALU.add
                                ).then_inc(emptied_sem(("gating", t)), 1)
                wait_emptied(dve, ("gating", t))
                wait_emptied(dve, ("uz", 0, t))
                V.tensor_tensor(cout[:, t, :], cout[:, t, :], uz[:, t, :], ALU.mult).then_inc(cout_ready, 1)
            dve.wait_ge(tabd_ready, 1)
            attention(attD)
            add_to_x("odout")
            feed_forward(1)
            normed("F2", rows_=row[:, LATE["final2"][0]:LATE["final2"][1]], signal=out_ready)



def t5_bucket(rel):
    nb, max_exact = 16, 8
    n = np.abs(rel)
    large = max_exact + (np.log(np.maximum(n, 1) / max_exact) / np.log(1024 / max_exact) * (nb - max_exact)).astype(np.int64)
    return (rel > 0) * nb + np.where(n < max_exact, n, np.minimum(large, nb - 1))


def shape_constants():
    c = np.zeros((P, NCONST), np.float32)

    def put(name, v):
        c[:, CONST[name][0]:CONST[name][1]] = v
    p = np.arange(P)[:, None]
    put("ident", np.eye(P))
    put("ones", 1.0)
    put("inv", np.power(np.float32(10000.0), -(np.arange(32, dtype=np.float32) * np.float32(2.0) / np.float32(64)))[None])
    rel = p - (np.arange(TABW)[None] - P)
    put("mask1", np.where((rel >= 0) & (rel < 128), 0.0, NEG))
    qc, kc = p % GRID, np.arange(GRID)[None]
    start = np.clip(qc - 8, 0, GRID - 16)
    put("namask", np.where((kc >= start) & (kc < start + 16), 0.0, NEG))
    inv = np.float32(1.0) / np.power(np.float32(10000.0), np.arange(0, ROPE2, 2, dtype=np.float32) / np.float32(ROPE2))
    ang = (np.arange(S, dtype=np.float32)[:, None] * inv[None]).reshape(NT, P, 16).transpose(1, 0, 2).reshape(P, 32)
    put("cos2", np.cos(ang))
    put("sin2", np.sin(ang))
    put("iota", np.arange(TOPK)[None])
    rel = np.arange(REL) - S
    t5 = np.zeros((32 + HEADS2, REL), np.float32)
    t5[t5_bucket(rel), np.arange(REL)] = 1.0
    count = (np.abs(rel) <= 64).astype(int) + (rel % 4 == 0) + (rel % 16 == 0)
    t5[32:] = np.where(count > 0, np.log(np.maximum(count, 1)), NEG)[None]
    return c, t5



def by_k(w):
    k, n = w.shape
    return w.reshape(k // P, P, n).transpose(1, 0, 2).reshape(P, -1)


def feature(v):
    return v.reshape(-1, P).T


def kernel(**inputs):
    import concourse.bacc as bacc
    from concourse.bass_utils import run_bass_kernel_spmd

    a = {k: np.asarray(v) for k, v in inputs.items()}
    w_in = a["w_in"][0]
    parts = {}
    for i in range(4):
        parts["glu", i] = by_k(np.concatenate([w_in[:, 256 * i:256 * i + 256], w_in[:, 1024 + 256 * i:1280 + 256 * i]], 1))
        parts["gate", i] = by_k(w_in[:, 3328 + 512 * i:3840 + 512 * i])
        parts["pq", i] = by_k(a["w_peer_q"][0][:, 512 * i:512 * i + 512])
    parts["kv1", 0] = by_k(w_in[:, 3072:3328])
    ev, od = a["ev_w_in_2"][0], a["od_w_in_2"][0]
    for i in range(2):
        c = slice(512 * i, 512 * i + 512)
        parts["q1", i] = by_k(w_in[:, 2048 + 512 * i:2560 + 512 * i])
        for name, w in (("convout", "w_conv_out"), ("attno", "w_attn_o"), ("wout", "w_out"), ("evout", "ev_w_out_2"),
                        ("odout", "od_w_out_2")):
            parts[name, i] = by_k(a[w][0][:, c])
        parts["cqkv", i] = by_k(ev[:, 1536 + 512 * i:2048 + 512 * i])
    parts["keys", 0] = a["peer_sub_keys"][0].transpose(3, 0, 1, 2).reshape(P, -1)
    for i, name in enumerate(("qa", "ka", "va")):
        parts[name, 0] = by_k(ev[:, 512 * i:512 * i + 512])
    w_uq = a["ev_w_uq_2"][0]
    parts["kpe_uq", 0] = np.concatenate([by_k(ev[:, 2560:2592]), by_k(w_uq[:, 0:512])], 1)
    parts["uq_ukv", 0] = np.concatenate([by_k(w_uq[:, 512:768]), by_k(a["ev_w_ukv_2"][0])], 1)
    for i, name in enumerate(("uz", "vz", "qd", "kd", "vd")):
        parts[name, 0] = by_k(od[:, 512 * i:512 * i + 512])
    parts["ws", 0] = a["od_w_s_2"][0].transpose(2, 0, 1).reshape(P, -1)
    for layer in range(2):
        gu, down = a["ffn_w_gu_2"][layer], a["ffn_w_down_2"][layer]
        for i in range(KF // 2):
            parts["gu%d" % layer, i] = by_k(np.concatenate([gu[:, 256 * i:256 * i + 256],
                                                            gu[:, FF + 256 * i:FF + 256 * i + 256]], 1))
        for i in range(-(-KF // 4)):
            parts["down%d" % layer, i] = by_k(down[512 * i:512 * i + 512])
    for name, width in CHUNKS:
        assert parts[name].shape == (P, width), (name, parts[name].shape, width)
    stream = np.concatenate([np.ascontiguousarray(parts[name]).ravel() for name, _ in CHUNKS])

    params = np.concatenate([
        feature(a["norm1_g"][0]), feature(a["b_in"][0][0:2048]), feature(a["b_in"][0][3328:5376]),
        a["conv_w"][0].reshape(TAPS, KD, P).transpose(2, 1, 0).reshape(P, -1), feature(a["conv_b"][0]),
        feature(a["conv_ln_g"][0]), feature(a["conv_ln_b"][0]), feature(a["norm_mix_2"][0]),
        feature(a["norm_mix_2"][1]), feature(a["norm_ffn_2"][0]), feature(a["norm_ffn_2"][1]),
        feature(a["ev_q_gain_2"][0]), feature(a["ev_kv_gain_2"][0]), a["od_b_s_2"][0].T], 1)
    rows = np.concatenate([a["b_in"][0][2048:3328], a["attn_sinks"][0], a["norm2_g"][0], a["final_g"]])[None]
    late = np.concatenate([a["final_gain_2"], a["od_v_gain_2"][0]])[None]
    uv = np.concatenate([a["peer_u"][0], a["peer_v"][0]], 1)
    consts, t5 = shape_constants()
    arrays = {
        "stream": stream, "consts": consts, "t5const": t5, "params": params, "rows": rows, "late_rows": late,
        "x_in": a["x"].reshape(S, D), "positions": a["positions"].reshape(NT, P).T, "t5_in": a["t5_bias_2"],
        "rpb_in": a["od_rpb_2"][0], "uv": uv,
    }
    nc = bacc.Bacc("TRN2", target_bir_lowering=False, num_devices=1)
    arrays = {k: np.ascontiguousarray(v) for k, v in arrays.items()}
    aps = {k: nc.dram_tensor(k, v.shape, mybir.dt.from_np(v.dtype), kind="ExternalInput").ap() for k, v in arrays.items()}
    out = nc.dram_tensor("out", (S, D), F32, kind="ExternalOutput").ap()
    build(nc, out=out, **aps)
    r = run_bass_kernel_spmd(nc, [arrays], core_ids=[0])
    return r.results[0]["out"].reshape(1, S, D)
```

```python
from contextlib import ExitStack

import numpy as np
import concourse.bass as bass
from concourse import mybir

F32 = mybir.dt.float32
F32R = mybir.dt.float32r
U32 = mybir.dt.uint32
I32 = mybir.dt.int32
ALU = mybir.AluOpType
ACT = mybir.ActivationFunctionType
AX = mybir.AxisListType.X

P = 128
S = 256
NT = S // P
D = 1024
KD = D // P
TAPS = 31
HD = 64
QH, KVH = 16, 2
PH, TOPK, NKEYS = 8, 16, 128
SLOTS = PH * TOPK
NEXP = NKEYS * NKEYS
FF = 2816
KF = FF // P
HEADS2 = 8
QRANK, KVRANK, NOPE, ROPE2 = 768, 256, 64, 32
QK2 = NOPE + ROPE2
CW = 512
GRID = 64
EPS = 1e-6
NEG = -1e30
UNIT_GROUPS = 2 * TOPK // 2
UNITS = NT * PH // 2
NSLOT = 3
SLOTW = 4096
RB = 6
REL = 2 * S
TABW = S + P



def columns(parts):
    at, out = 0, {}
    for name, n in parts:
        out[name] = (at, at + n)
        at += n
    return out, at


CONST, NCONST = columns([("ident", 128), ("ones", 128), ("inv", 32), ("mask1", TABW), ("namask", GRID),
                         ("cos2", 32), ("sin2", 32), ("iota", 16)])
PARAM, NPARAM = columns([("norm1", 8), ("b_glu", 16), ("b_gate", 16), ("conv_w", KD * TAPS), ("conv_b", 8),
                         ("ln_g", 8), ("ln_b", 8), ("mix0", 8), ("mix1", 8), ("ffn0", 8), ("ffn1", 8),
                         ("qkv_gain", 8), ("b_s", 8)])
ROW, NROW = columns([("b_qkv", 1280), ("sinks", 16), ("norm2", D), ("final1", D)])
LATE = {"final2": (0, D), "v_gain": (1296, 1296 + CW)}
RPB_ROWS = 7



def chunk_list():
    out = [(("glu", i), 4096) for i in range(4)] + [(("q1", i), 4096) for i in range(2)] + [(("kv1", 0), 2048)]
    out += [(("gate", i), 4096) for i in range(4)]
    out += [(("convout", i), 4096) for i in range(2)] + [(("attno", i), 4096) for i in range(2)]
    out += [(("wout", i), 4096) for i in range(2)]
    out += [(("pq", i), 4096) for i in range(4)]
    out += [(("qa", 0), 4096), (("ka", 0), 4096), (("va", 0), 4096), (("cqkv", 0), 4096), (("cqkv", 1), 4096),
            (("kpe_uq", 0), 3328), (("uq_ukv", 0), 3584), (("evout", 0), 4096), (("evout", 1), 4096)]
    for layer in range(2):
        if layer:
            out += [(("uz", 0), 4096), (("vz", 0), 4096), (("qd", 0), 4096), (("kd", 0), 4096), (("vd", 0), 4096),
                    (("ws", 0), 1024), (("odout", 0), 4096), (("odout", 1), 4096)]
        out += [(("gu%d" % layer, i), 4096) for i in range(KF // 2)]
        out += [(("down%d" % layer, i), min(4, KF - 4 * i) * D) for i in range(-(-KF // 4))]
    return out


CHUNKS = chunk_list()
CHUNK_NO = {name: n for n, (name, _) in enumerate(CHUNKS)}
CHUNK_AT = np.cumsum([0] + [P * w for _, w in CHUNKS]).tolist()



def attention_fills(a, heads):
    out = [(a, "S", 0), (a, "S", 1)]
    for h in range(heads):
        out.append((a, "T", h))
        if h + 2 < heads:
            out.append((a, "S", h + 2))
    return out + [(a, "OT", g, t) for g in range(heads // 8) for t in range(NT)]


def norm_fills(name):
    return [(name, t, half) for t in range(NT) for half in range(2)]


def tm_fills(name, chunks=1):
    return [(name, i, t) for i in range(chunks) for t in range(NT)]


def fm_fills(name, chunks=1):
    return [(name, i, pair) for i in range(chunks) for pair in range(2)]


QUERY_ORDER = [("pq", 0), ("pq", 1), ("sc", 0), ("pq", 2), ("sc", 1), ("pq", 3), ("sc", 2), ("sc", 3)]


def fill_list():
    out = [("t5",)] + norm_fills("N1") + fm_fills("glu", 4) + tm_fills("q1", 2) + tm_fills("kv1")
    out += fm_fills("gate", 4)
    out += [("q1T", t, half) for t in range(NT) for half in range(2)] + [("k1T",), ("mean",), ("var",)]
    out += attention_fills("att1", QH)
    out += fm_fills("convout", 2) + fm_fills("attno", 2) + tm_fills("wout", 2)
    out += norm_fills("N2")
    for kind, i in QUERY_ORDER:
        out += [(kind, i, j) for j in range(2)]
    out += norm_fills("mix0") + fm_fills("qa") + fm_fills("ka") + tm_fills("va") + tm_fills("cqkv", 2)
    out += attention_fills("attA", HEADS2)
    out += norm_fills("cT") + tm_fills("kpe") + tm_fills("uqa") + tm_fills("uqb") + tm_fills("ukv", 2)
    out += [(n, t, half) for n in ("qmT", "kmT") for t in range(NT) for half in range(2)]
    out += attention_fills("attB", HEADS2) + tm_fills("evout", 2)
    for layer in range(2):
        if layer:
            out += norm_fills("mix1") + tm_fills("uz") + tm_fills("vz") + fm_fills("qd") + fm_fills("kd")
            out += tm_fills("vd") + [("gating", t) for t in range(NT)] + [("coutT", t) for t in range(NT)]
            out += attention_fills("attD", HEADS2) + tm_fills("odout", 2)
        out += norm_fills("ffn%d" % layer) + fm_fills("gu%d" % layer, KF // 2)
        out += [("down%d" % layer, half, t) for half in range(2) for t in range(NT)]
    return out


FILLS = fill_list()
FILL_NO = {name: n for n, name in enumerate(FILLS)}
assert len(FILL_NO) == len(FILLS)

LAST_USE = {("kpe_uq", 0): ("uqa", 0, 1), ("uq_ukv", 0): ("ukv", 1, 1),
            ("ws", 0): ("gating", 1)}


PROJECTIONS = (("qa", "ka", "va", ("cqkv", 0), ("cqkv", 1)), ("uz", "vz", "qd", "kd", "vd"))
PROJECTIONS = [[c if isinstance(c, tuple) else (c, 0) for c in cs] for cs in PROJECTIONS]
FEATURE_MAJOR = ("qa", "ka", "qd", "kd")
GU, DOWN, LAYER_PARTS = 10, 10 + KF, 10 + KF + KF // 2


def part_chunk(layer, q):
    if q < GU:
        return PROJECTIONS[layer][q // 2], q % 2
    if q < DOWN:
        return ("gu%d" % layer, (q - GU) // 2), q % 2
    return ("down%d" % layer, (q - DOWN) // 2), q % 2


def part_end(layer, q):
    (name, i), side = part_chunk(layer, q)
    if q < GU and name not in FEATURE_MAJOR:
        return (name, i, 1) if side else None
    if q < DOWN:
        return (name, i, side)
    return (name, 1, 1) if q == LAYER_PARTS - 1 else None


PARTS = [(layer, q) for layer in range(2) for q in range(LAYER_PARTS)]
PART_READ = {p: n + 1 for n, p in enumerate([p for p in PARTS if part_end(*p) is None])}
CHUNK_SPLIT = {part_chunk(*p)[0]: n + 1 for n, p in enumerate(PARTS)}


def last_use(chunk):
    return LAST_USE.get(chunk, (chunk[0], chunk[1], 1))



class Attention:
    def __init__(self, name, heads, q, k, v, scale, table, sinks, column):
        self.name, self.heads, self.q, self.k, self.v = name, heads, q, k, v
        self.scale, self.table, self.sinks, self.column = scale, table, sinks, column


def build(nc, stream, consts, t5const, params, rows, keys_in, late_rows, x_in, positions, t5_in, rpb_in, uv, out):
    with ExitStack() as ctx:
        def sb(name, shape, dt=F32):
            return ctx.enter_context(nc.sbuf_tensor(name, shape, dt))

        def sem(name):
            return ctx.enter_context(nc.semaphore(name))

        ring = sb("ring", [P, NSLOT, SLOTW])
        cst = sb("cst", [P, NCONST])
        par = sb("par", [P, NPARAM])
        row = sb("row", [P, NROW])
        x = sb("x", [P, NT, D])
        hT = sb("hT", [P, KD, S])
        xn = sb("xn", [P, NT, D])
        arena = nc.sbuf_base
        pool = sb("pool", [P, 16384])
        att = sb("att", [P, 7168])
        assert nc.sbuf_base == arena + 4 * (16384 + 7168)

        def rounded(name, at, shape):
            return nc.alloc_sbuf_tensor_at(name, shape, F32R, offset=arena + 4 * at)
        p_hi = rounded("p_hi", 6144, [P, KD, S])
        p_lo = rounded("p_lo", 8192, [P, KD, S])
        h_hi = rounded("h_hi", 0, [P, KD, S])
        h_lo = rounded("h_lo", 2048, [P, KD, S])
        gu_hi = rounded("gu_hi", 4096, [P, KF, S])
        gu_lo = rounded("gu_lo", 9728, [P, KF, S])
        w_hi = rounded("w_hi", 15360, [P, 2, 2048])
        w_lo = rounded("w_lo", 19456, [P, 2, 2048])
        tab = sb("tab", [P, HEADS2, TABW])
        small = sb("small", [P, 64])
        ssq = small[:, 0:2]
        rstd = small[:, 32:36]
        eps = small[:, 4:5]
        posf = small[:, 6:8]
        nsink = small[:, 8:24]
        vsum = small[:, 24:26]
        pos_i = sb("pos_i", [P, NT], I32)
        nmax = sb("nmax", [P, QH, NT])
        den = sb("den", [P, QH, NT])
        sinkw = sb("sinkw", [P, QH, NT])
        kpe = sb("kpe", [P, NT, ROPE2])
        angles = sb("angles", [P, 4, NT, 32])
        topv = sb("topv", [P, 4, TOPK])
        topi = sb("topi", [P, 4, TOPK], U32)
        topf = sb("topf", [P, 4, TOPK])
        best = sb("best", [P, 2, TOPK])
        bpos = sb("bpos", [P, 2, TOPK], U32)
        bdig = sb("bdig", [P, 2, 2, TOPK], U32)
        bdigf = sb("bdigf", [P, 2, 2, TOPK])
        hits = sb("hits", [P, 2, 2, TOPK])
        gsum = sb("gsum", [P, 2])
        gates = sb("gates", [P, NT * SLOTS])
        experts = sb("experts", [P, NT * SLOTS], U32)
        stage = sb("stage", [P, 4, 2], U32)
        pause = sb("pause", [1, 2])
        dots = sb("dots", [P, 4, 2])
        acts = sb("acts", [P, 4, 2])
        coef = sb("coef", [P, 4, 2])

        def view(base, at, *shape):
            n = int(np.prod(shape))
            v = base[:, at:at + n]
            if len(shape) == 2:
                return v.rearrange("p (a b) -> p a b", a=shape[0])
            if len(shape) == 3:
                return v.rearrange("p (a b c) -> p a b c", a=shape[0], b=shape[1])
            return v

        def c_(name):
            return cst[:, CONST[name][0]:CONST[name][1]]

        def par_(name):
            return par[:, PARAM[name][0]:PARAM[name][1]]

        def row_(name):
            return row[:, ROW[name][0]:ROW[name][1]]

        ident, ones = c_("ident"), c_("ones")
        conv_w = par_("conv_w").rearrange("p (k w) -> p k w", k=KD)
        sc_sb = view(att, 0, 2, 512)
        pr_sb = view(att, 1024, 2, 512)
        pt_sb = view(att, 2048, 2, 512)
        otm = view(att, 3072, NT, D)
        oT = view(att, 5120, KD, S)
        rope_tmp = view(att, 3072, 4, 18, 32)
        u = view(pool, 0, KD, TAPS - 1 + S)
        y = view(pool, 2288, KD, S)
        sgc = view(pool, 4336, KD, S)
        sga = view(pool, 6384, KD, S)
        qkv = view(pool, 8432, NT, 1280)
        qkr = view(pool, 10992, NT, 18 * HD)
        q1T = view(pool, 13296, KD, S)
        k1T = view(pool, 15344, KVH, S)
        kdup = pool[:, 15856:16368].rearrange("p (t n c d) -> p t n c d", t=NT, n=KVH, c=2)
        glu_sig = view(pool, 13296, 2, 512)
        ysq = view(att, 5120, KD, S)
        qpT = view(att, 5120, 2, 4, S)
        keys = tab[:, :, :].rearrange("p h j -> p (h j)")[:, 0:2048].rearrange("p (m n) -> p m n", n=NKEYS)
        gath = view(pool, 0, 8, 2 * D)
        scores = view(att, 0, NT, 2 * PH * NKEYS)
        cand = view(att, 4096, 2, TOPK * TOPK)
        qaT = view(pool, 0, 4, S)
        kaT = view(pool, 1024, 4, S)
        va = view(pool, 2048, NT, 512)
        cqkv = view(pool, 3072, NT, D)
        cT = view(pool, 5120, KD, S)
        uq = view(pool, 7168, NT, QRANK)
        ukv = view(pool, 8704, NT, D)
        km = view(pool, 10752, NT, HEADS2 * QK2)
        qmT = view(pool, 12288, HEADS2, S)
        kmT = view(pool, 14336, HEADS2, S)
        uz = view(pool, 0, NT, CW)
        vz = view(pool, 1024, NT, CW)
        qdT = view(pool, 2048, 4, S)
        kdT = view(pool, 3072, 4, S)
        vd = view(pool, 4096, NT, 512)
        cout = view(pool, 5120, NT, CW)
        silu = xn[:, 0, :].rearrange("p (b n) -> p b n", b=2)
        t5hot = att[0:32, 3072:3072 + REL]
        t5tab = att[0:32, 3584:3584 + HEADS2]
        t5ln = att[0:HEADS2, 3600:3600 + REL]
        t5vec = att[0:HEADS2, 4112:4112 + REL]
        rpb_pad = att[0:HEADS2, 4624:4624 + 15 * 128]

        t5_dram = nc.dram_tensor("t5_scratch", (HEADS2, P, REL), F32, kind="Internal").ap()
        rpb_dram = nc.dram_tensor("rpb_scratch", (HEADS2, RPB_ROWS, GRID, P), F32, kind="Internal").ap()

        psum = ctx.enter_context(nc.psum_tensor("psum", [P, 8, 512], F32))

        bank_filled = sem("bank_filled")
        bank_emptied = [sem("bank_emptied%d" % b) for b in range(RB)]
        chunk_landed = [sem("chunk_landed%d" % s) for s in range(NSLOT)]
        part_read = sem("part_read")
        hi_split = sem("hi_split")
        lo_split = sem("lo_split")
        h_split = sem("h_split")
        gu_ready = sem("gu_ready")
        const_landed = sem("const_landed")
        param_landed = sem("param_landed")
        x_landed = sem("x_landed")
        row_landed = sem("row_landed")
        keys_landed = sem("keys_landed")
        pos_landed = sem("pos_landed")
        t5_landed = sem("t5_landed")
        rpb_landed = sem("rpb_landed")
        rpb_cleared = sem("rpb_cleared")
        t5_stored = sem("t5_stored")
        rpb_stored = sem("rpb_stored")
        taba_landed = sem("taba_landed")
        tabd_landed = sem("tabd_landed")
        tabd_ready = sem("tabd_ready")
        late_landed = sem("late_landed")
        vector_step = sem("vector_step")
        scalar_step = sem("scalar_step")
        eps_ready = sem("eps_ready")
        root_ready = sem("root_ready")
        x_normed = sem("x_normed")
        xn_ready = sem("xn_ready")
        angle_ready = sem("angle_ready")
        trig_ready = sem("trig_ready")
        conv_ready = sem("conv_ready")
        ysq_ready = sem("ysq_ready")
        ynorm_ready = sem("ynorm_ready")
        silu_ready = sem("silu_ready")
        rope_ready = sem("rope_ready")
        nmax_ready = sem("nmax_ready")
        probs_ready = sem("probs_ready")
        pv_done = sem("pv_done")
        nmaxs_ready = sem("nmaxs_ready")
        sinkw_ready = sem("sinkw_ready")
        o_emptied = sem("o_emptied")
        merged_ready = sem("merged_ready")
        shifted_ready = sem("shifted_ready")
        best_exp_ready = sem("best_exp_ready")
        selected = sem("selected")
        stage_ready = sem("stage_ready")
        rows_landed = [sem("rows_landed%d" % b) for b in range(4)]
        rows_used = sem("rows_used")
        dots_ready = sem("dots_ready")
        acts_ready = sem("acts_ready")
        vcen_ready = sem("vcen_ready")
        vroot_ready = sem("vroot_ready")
        vn_ready = sem("vn_ready")
        cout_ready = sem("cout_ready")
        out_ready = sem("out_ready")
        out_stored = sem("out_stored")

        def bank(name):
            return psum[:, FILL_NO[name] % RB, :]

        def wait_filled(eng, name):
            eng.wait_ge(bank_filled, FILL_NO[name] + 1)
            return bank(name)

        def emptied_sem(name):
            return bank_emptied[FILL_NO[name] % RB]

        def wait_emptied(eng, name):
            eng.wait_ge(emptied_sem(name), FILL_NO[name] // RB + 1)

        def wait_chunk(eng, name):
            n = CHUNK_NO[name]
            eng.wait_ge(chunk_landed[n % NSLOT], 16 * (n // NSLOT + 1))
            return ring[:, n % NSLOT, :]

        def part_raw(layer, q):
            chunk, side = part_chunk(layer, q)
            w = ring[:, CHUNK_NO[chunk] % NSLOT, :]
            if q < DOWN:
                return w.rearrange("p (k n) -> p k n", k=KD)[:, :, 256 * side:256 * side + 256]
            return w[:, 2048 * side:2048 * side + 2048].rearrange("p (k n) -> p k n", k=KD)

        def part_split(tensor, layer, q):
            return tensor[:, (LAYER_PARTS * layer + q) % 2, :].rearrange("p (k n) -> p k n", k=KD)

        def wait_part_used(eng, layer, q):
            if part_end(layer, q) is not None:
                eng.wait_ge(bank_filled, FILL_NO[part_end(layer, q)] + 1)
            else:
                eng.wait_ge(part_read, PART_READ[layer, q])

        def half(h):
            return slice(HD * (h % 2), HD * (h % 2) + HD)

        def tile128(t):
            return slice(P * t, P * t + P)

        att1 = Attention(
            "att1", QH, lambda h, t: q1T[half(h), h // 2, tile128(t)], lambda h: k1T[half(h), h // (QH // KVH), :],
            lambda h, kt: qkv[:, kt, 1152 + HD * (h // 8):1152 + HD * (h // 8) + HD],
            HD ** -0.5, lambda h: c_("mask1"), True, lambda g: 512 * g)
        attA = Attention(
            "attA", HEADS2, lambda h, t: qaT[half(h), h // 2, tile128(t)], lambda h: kaT[half(h), h // 2, :],
            lambda h, kt: va[:, kt, HD * h:HD * h + HD], HD ** -0.5, lambda h: tab[:, h, :], False, lambda g: 0)
        attB = Attention(
            "attB", HEADS2, lambda h, t: qmT[0:QK2, h, tile128(t)], lambda h: kmT[0:QK2, h, :],
            lambda h, kt: ukv[:, kt, P * h + NOPE:P * h + P], QK2 ** -0.5, None, False, lambda g: 512)
        attD = Attention(
            "attD", HEADS2, lambda h, t: qdT[half(h), h // 2, tile128(t)], lambda h: kdT[half(h), h // 2, :],
            lambda h, kt: vd[:, kt, HD * h:HD * h + HD], HD ** -0.5, lambda h: tab[:, h, :], False, lambda g: 512)
        first_head = {"att1": 0, "attA": QH, "attB": QH + HEADS2, "attD": QH + 2 * HEADS2}
        gain_of = {"N1": "norm1", "mix0": "mix0", "mix1": "mix1", "ffn0": "ffn0", "ffn1": "ffn1", "cT": "qkv_gain"}
        first_probs = {"att1": 0, "attA": QH, "attD": QH + HEADS2}
        first_group = {"att1": 0, "attA": 2, "attB": 3, "attD": 4}

        def wait_probs(eng, a, h):
            if a.table is None:
                wait_emptied(eng, (a.name, "S", h))
            else:
                eng.wait_ge(probs_ready, first_probs[a.name] + h + 1)

        roots_before = {"N1": 0, "N2": 2, "F1": 4, "mix0": 6, "cT": 8, "ffn0": 12, "mix1": 14, "ffn1": 16, "F2": 18}
        xn_before = {"N1": 0, "N2": 2, "mix0": 4, "cT": 6, "ffn0": 8, "mix1": 10, "ffn1": 12}

        block = ctx.enter_context(nc.Block())

        @block.sync
        def _(sp):
            sp.dma_start(x[:, :, :], x_in.rearrange("(t p) d -> p t d", p=P)).then_inc(x_landed, 16)
            sp.dma_start(cst[:, :], consts).then_inc(const_landed, 16)
            sp.dma_start(par[:, :], params).then_inc(param_landed, 16)
            for n, (name, width) in enumerate(CHUNKS):
                if n >= NSLOT:
                    before = CHUNKS[n - NSLOT][0]
                    if before in CHUNK_SPLIT:
                        sp.wait_ge(lo_split, CHUNK_SPLIT[before])
                    else:
                        sp.wait_ge(bank_filled, FILL_NO[last_use(before)] + 1)
                src = stream[CHUNK_AT[n]:CHUNK_AT[n + 1]].rearrange("(p w) -> p w", p=P)
                sp.dma_start(ring[:, n % NSLOT, 0:width], src).then_inc(chunk_landed[n % NSLOT], 16)
            for t in range(NT):
                sp.wait_ge(out_ready, t + 1)
                sp.dma_start(out[P * t:P * t + P, :], xn[:, t, :]).then_inc(out_stored, 16)
            sp.wait_ge(out_stored, 16 * NT)

        @block.gpsimd
        def _(gp):
            gp.dma_start(pos_i[:, :], positions).then_inc(pos_landed, 16)
            gp.dma_start(t5hot, t5const[0:32, :]).then_inc(t5_landed, 16)
            gp.dma_start(t5ln, t5const[32:32 + HEADS2, :]).then_inc(t5_landed, 16)
            gp.dma_start(t5tab, t5_in).then_inc(t5_landed, 16)
            gp.dma_start(row[:, :], rows.to_broadcast([P, NROW])).then_inc(row_landed, 16)
            gp.dma_start(keys.rearrange("p m n -> p (m n)"), keys_in).then_inc(keys_landed, 16)
            nc.gpsimd.memset(pause[:, :], 0.0).then_inc(rpb_cleared, 1)
            nc.gpsimd.memset(rpb_pad, 0.0).then_inc(rpb_cleared, 1)
            gp.wait_ge(rpb_cleared, 2)
            rp = rpb_pad.rearrange("h (r c) -> h r c", r=15)
            gp.dma_start(rp[:, :, 48:79], rpb_in).then_inc(rpb_landed, 16)
            gp.wait_ge(rpb_landed, 16)
            for r in range(RPB_ROWS):
                gp.dma_start(rpb_dram[:, r], rp[:, r + 4, :].unsqueeze(1).to_broadcast([HEADS2, GRID, P])
                             ).then_inc(rpb_stored, 16)
            wait_emptied(gp, ("t5",))
            gp.dma_start(t5_dram, t5vec.unsqueeze(1).to_broadcast([HEADS2, P, REL])).then_inc(t5_stored, 16)
            gp.wait_ge(t5_stored, 16)
            gp.wait_ge(rpb_stored, 16 * RPB_ROWS)

            def gather(n, b, r, fresh):
                if not fresh:
                    gp.wait_ge(rows_used, r * 4 + (n + b - 3))
                nc.gpsimd.tensor_copy(stage[:, b, :], experts[:, bass.ds(r * 8 + 2 * (n + b), 2)]
                                      ).then_inc(stage_ready, 1)
                gp.wait_ge(stage_ready, r * 4 + (n + b + 1))
                nc.gpsimd.tensor_tensor(pause[:, 1:2], pause[:, 0:1], pause[:, 0:1], ALU.add)
                for k in range(2):
                    gp.indirect_dma_start(out=gath[:, 2 * b + k, :], out_offset=None, in_=uv,
                                          in_offset=bass.IndirectOffsetOnAxis(ap=stage[:, b, k:k + 1], axis=0)
                                          ).then_inc(rows_landed[b], 16)

            for unit in range(UNITS):
                gp.wait_ge(selected, unit + 1)
                if unit == 0:
                    for b in range(4):
                        gather(0, b, 0, True)
                if unit == 1:
                    gp.wait_ge(bank_filled, FILL_NO[("sc", 3, 1)] + 1)
                    gp.dma_start(tab[:, :, :], bass.AP(tensor=t5_dram.tensor, offset=S - P,
                                                       ap=[[REL - 1, P], [P * REL, HEADS2], [1, TABW]])
                                 ).then_inc(taba_landed, 16)
                with gp.Fori(1 if unit == 0 else 0, UNIT_GROUPS // 4) as r:
                    for b in range(4):
                        gather(UNIT_GROUPS * unit, b, r, False)

            gp.wait_ge(bank_filled, FILL_NO[("attA", "OT", 0, 0)] + 1)
            for qr in range(2):
                for h in range(HEADS2):
                    gp.dma_start(tab[GRID * qr:GRID * qr + GRID, h, :].rearrange("p (r c) -> p r c", r=6),
                                 bass.AP(tensor=rpb_dram.tensor, offset=(h * RPB_ROWS + 1 - qr) * GRID * P + GRID - 1,
                                         ap=[[P - 1, GRID], [GRID * P, 6], [1, GRID]])).then_inc(tabd_landed, 16)
            gp.dma_start(row[:, LATE["final2"][0]:LATE["final2"][1]],
                         late_rows[:, 0:D].to_broadcast([P, D])).then_inc(late_landed, 16)
            gp.dma_start(row[:, LATE["v_gain"][0]:LATE["v_gain"][1]],
                         late_rows[:, D:D + CW].to_broadcast([P, CW])).then_inc(late_landed, 16)
            gp.wait_ge(tabd_landed, 16 * 2 * HEADS2)
            blocks = tab[:, :, :].rearrange("p h (r c) -> p (h r) c", c=GRID)
            nc.gpsimd.tensor_tensor(blocks, blocks, c_("namask").unsqueeze(1).to_broadcast([P, 6 * HEADS2, GRID]),
                                    ALU.add).then_inc(tabd_ready, 1)

        @block.tensor
        def _(pe):
            filled_so_far = [0]

            def begin(name):
                n = FILL_NO[name]
                assert n == filled_so_far[0], (name, FILLS[filled_so_far[0]])
                filled_so_far[0] += 1
                if n >= RB:
                    pe.wait_ge(bank_emptied[n % RB], n // RB)
                return bank(name)

            def accumulate(dst, pairs):
                for i, (lhsT, rhs) in enumerate(pairs):
                    last = nc.tensor.matmul(dst, lhsT, rhs, start=(i == 0), stop=(i == len(pairs) - 1))
                return last

            def feature_major_chunk(name, i, act):
                w = wait_chunk(pe, (name, i))[:, 0:4096].rearrange("p (k n) -> p k n", k=KD)
                for pair in range(2):
                    dst = begin((name, i, pair))
                    for j in range(2):
                        c = P * (2 * pair + j)
                        last = accumulate(dst[:, S * j:S * j + S], [(w[:, k, c:c + P], act[:, k, :]) for k in range(KD)])
                    last.then_inc(bank_filled, 1)

            def feature_major(name, chunks, act=None):
                for i in range(chunks):
                    feature_major_chunk(name, i, hT if act is None else act)

            def token_major(name, i, w, act, kd, n):
                for t in range(NT):
                    dst = begin((name, i, t))
                    accumulate(dst[:, 0:n], [(act[:, k, tile128(t)], w[:, k, :]) for k in range(kd)]
                               ).then_inc(bank_filled, 1)

            def token_major_chunks(name, chunks, act, n=512):
                for i in range(chunks):
                    w = wait_chunk(pe, (name, i))[:, 0:KD * n].rearrange("p (k n) -> p k n", k=KD)
                    token_major(name, i, w, act, KD, n)

            def transposes(name, sources, rows_out=P):
                dst = begin(name)
                for j, src in enumerate(sources):
                    last = nc.tensor.transpose(dst[0:rows_out, P * j:P * j + P], src, ident)
                last.then_inc(bank_filled, 1)

            def norm_transposes(name, src):
                for t in range(NT):
                    pe.wait_ge(xn_ready, xn_before[name] + t + 1)
                    for hf in range(2):
                        transposes((name, t, hf), [src[:, t, P * k:P * k + P] for k in range(4 * hf, 4 * hf + 4)])
                for t in range(NT):
                    for hf in range(2):
                        wait_emptied(pe, (name, t, hf))

            def attention(a):
                def scores_of(h):
                    dst = begin((a.name, "S", h))
                    for t in range(NT):
                        last = nc.tensor.matmul(dst[:, S * t:S * t + S], a.q(h, t), a.k(h), start=True, stop=True)
                    last.then_inc(bank_filled, 1)

                def turn(h):
                    wait_probs(pe, a, h)
                    transposes((a.name, "T", h), [pr_sb[:, h % 2, S * t + P * kt:S * t + P * kt + P]
                                                  for kt in range(NT) for t in range(NT)])

                def values(h):
                    g = first_group[a.name] + h // 8
                    if h % 8 == 0 and g > 0:
                        pe.wait_ge(o_emptied, NT * g)
                    wait_emptied(pe, (a.name, "T", h))
                    c = HD * (h % 8)
                    for t in range(NT):
                        last = accumulate(psum[:, RB + t, c:c + HD],
                                          [(pt_sb[:, h % 2, S * kt + P * t:S * kt + P * t + P], a.v(h, kt))
                                           for kt in range(NT)])
                    last.then_inc(pv_done, 1)

                scores_of(0)
                scores_of(1)
                for h in range(a.heads):
                    turn(h)
                    if h + 2 < a.heads:
                        scores_of(h + 2)
                    if h:
                        values(h - 1)
                values(a.heads - 1)
                for g in range(a.heads // 8):
                    for t in range(NT):
                        pe.wait_ge(o_emptied, NT * (first_group[a.name] + g) + t + 1)
                        c = a.column(g)
                        transposes((a.name, "OT", g, t), [otm[:, t, c + P * j:c + P * j + P] for j in range(4)])

            def wait_turned(a):
                for g in range(a.heads // 8):
                    for t in range(NT):
                        wait_emptied(pe, (a.name, "OT", g, t))

            def split_products(dst, lhsT, rhs, start, stop):
                nc.tensor.matmul(dst, lhsT[0], rhs[0], start=start, stop=False)
                nc.tensor.matmul(dst, lhsT[0], rhs[1], start=False, stop=False)
                return nc.tensor.matmul(dst, lhsT[1], rhs[0], start=False, stop=stop)

            def wait_part(layer, q):
                pe.wait_ge(lo_split, LAYER_PARTS * layer + q + 1)
                return [part_split(v, layer, q) for v in (w_hi, w_lo)]

            def split_feature_major(layer, q, halves):
                w = wait_part(layer, q)
                dst = begin(part_end(layer, q))
                for j in range(2):
                    for k in range(KD):
                        last = split_products(dst[:, S * j:S * j + S], [v[:, k, P * j:P * j + P] for v in w],
                                              [v[:, k, :] for v in halves], k == 0, k == KD - 1)
                last.then_inc(bank_filled, 1)

            def projections(layer):
                pe.wait_ge(h_split, 4 * 2 * layer + 4)
                for c, (name, i) in enumerate(PROJECTIONS[layer]):
                    if name in FEATURE_MAJOR:
                        for q in (2 * c, 2 * c + 1):
                            split_feature_major(layer, q, (p_hi, p_lo))
                        continue
                    banks = [begin((name, i, t)) for t in range(NT)]
                    for side in range(2):
                        w = wait_part(layer, 2 * c + side)
                        for t in range(NT):
                            for k in range(KD):
                                last = split_products(banks[t][:, 256 * side:256 * side + 256],
                                                      [v[:, k, tile128(t)] for v in (p_hi, p_lo)],
                                                      [v[:, k, :] for v in w], k == 0, k == KD - 1)
                            if side:
                                last.then_inc(bank_filled, 1)
                        if not side:
                            last.then_inc(part_read, 1)

            def feed_forward(layer):
                norm_transposes("ffn%d" % layer, xn)
                pe.wait_ge(h_split, 4 * (2 * layer + 1) + 4)
                for q in range(GU, DOWN):
                    split_feature_major(layer, q, (h_hi, h_lo))
                banks = {(n, t): begin(("down%d" % layer, n, t)) for n in range(2) for t in range(NT)}
                for q in range(DOWN, LAYER_PARTS):
                    j = q - DOWN
                    w = [v.rearrange("p k n -> p (k n)") for v in wait_part(layer, q)]
                    pe.wait_ge(gu_ready, KF // 2 * layer + j + 1)
                    for k in (2 * j, 2 * j + 1):
                        for n in range(2):
                            for t in range(NT):
                                c = D * (k % 2) + 512 * n
                                last = split_products(banks[n, t], [v[:, k, tile128(t)] for v in (gu_hi, gu_lo)],
                                                      [v[:, c:c + 512] for v in w], k == 0, k == KF - 1)
                                if k == KF - 1:
                                    last.then_inc(bank_filled, 1)
                    if q < LAYER_PARTS - 1:
                        last.then_inc(part_read, 1)

            pe.wait_ge(t5_landed, 48)
            nc.tensor.matmul(begin(("t5",))[0:HEADS2, :], t5tab, t5hot, start=True, stop=True).then_inc(bank_filled, 1)

            pe.wait_ge(const_landed, 16)
            norm_transposes("N1", xn)
            feature_major("glu", 4)
            token_major_chunks("q1", 2, hT)
            token_major_chunks("kv1", 1, hT, 256)
            feature_major("gate", 4)
            for t in range(NT):
                pe.wait_ge(rope_ready, t + 1)
                for hf in range(2):
                    transposes(("q1T", t, hf), [qkr[:, t, P * k:P * k + P] for k in range(4 * hf, 4 * hf + 4)])
            transposes(("k1T",), [kdup[:, t, n].rearrange("p c d -> p (c d)") for n in range(KVH) for t in range(NT)])
            pe.wait_ge(conv_ready, 4)
            accumulate(begin(("mean",))[:, 0:S], [(ones, y[:, k, :]) for k in range(KD)]).then_inc(bank_filled, 1)
            pe.wait_ge(ysq_ready, 1)
            accumulate(begin(("var",))[:, 0:S], [(ones, ysq[:, k, :]) for k in range(KD)]).then_inc(bank_filled, 1)
            for t in range(NT):
                for hf in range(2):
                    wait_emptied(pe, ("q1T", t, hf))
                wait_emptied(pe, ("kv1", 0, t))
            wait_emptied(pe, ("k1T",))
            attention(att1)
            pe.wait_ge(silu_ready, 1)
            feature_major("convout", 2, y)
            wait_turned(att1)
            feature_major("attno", 2, oT)
            pe.wait_ge(merged_ready, 1)
            token_major_chunks("wout", 2, hT)
            norm_transposes("N2", xn)
            pe.wait_ge(keys_landed, 16)
            for kind, i in QUERY_ORDER:
                if kind == "pq":
                    feature_major_chunk(kind, i, hT)
                    continue
                for pair in range(2):
                    wait_emptied(pe, ("pq", i, pair))
                for t in range(NT):
                    dst = begin(("sc", i, t))
                    for m in range(4):
                        last = nc.tensor.matmul(dst[:, NKEYS * m:NKEYS * m + NKEYS], qpT[:, i % 2, m, tile128(t)],
                                                keys[:, 4 * i + m, :], start=True, stop=True)
                    last.then_inc(bank_filled, 1)

            norm_transposes("mix0", xn)
            projections(0)
            for name in ("qa", "ka"):
                for pair in range(2):
                    wait_emptied(pe, (name, 0, pair))
            for t in range(NT):
                wait_emptied(pe, ("va", 0, t))
            attention(attA)
            norm_transposes("cT", cqkv)
            w = wait_chunk(pe, ("kpe_uq", 0))
            token_major("kpe", 0, w[:, 0:256].rearrange("p (k n) -> p k n", k=KD), hT, KD, ROPE2)
            token_major("uqa", 0, w[:, 256:3328].rearrange("p (k n) -> p k n", k=6), cT, 6, 512)
            w = wait_chunk(pe, ("uq_ukv", 0))
            token_major("uqb", 0, w[:, 0:1536].rearrange("p (k n) -> p k n", k=6), cT, 6, 256)
            for i in range(2):
                token_major("ukv", i, w[:, 1536:3584].rearrange("p (k n) -> p k n", k=2)[:, :, 512 * i:512 * i + 512],
                            cT[:, 6:8, :], 2, 512)
            for n, src in (("qmT", uq), ("kmT", km)):
                for t in range(NT):
                    pe.wait_ge(rope_ready, NT + t + 1)
                    for hf in range(2):
                        transposes((n, t, hf), [src[:, t, QK2 * h:QK2 * h + QK2] for h in range(4 * hf, 4 * hf + 4)],
                                   QK2)
            for n in ("qmT", "kmT"):
                for t in range(NT):
                    for hf in range(2):
                        wait_emptied(pe, (n, t, hf))
            for i in range(2):
                for t in range(NT):
                    wait_emptied(pe, ("ukv", i, t))
            attention(attB)
            wait_turned(attA)
            wait_turned(attB)
            token_major_chunks("evout", 2, oT)

            feed_forward(0)
            norm_transposes("mix1", xn)
            projections(1)
            ws = wait_chunk(pe, ("ws", 0))[:, 0:1024].rearrange("p (g i) -> p g i", g=8)
            for t in range(NT):
                pe.wait_ge(vn_ready, t + 1)
                dst = begin(("gating", t))
                for g in range(8):
                    last = nc.tensor.matmul(dst[:, 64 * g:64 * g + 64], ws[:, g, :], vz[:, t, 64 * g:64 * g + 64],
                                            start=True, stop=True)
                last.then_inc(bank_filled, 1)
            for t in range(NT):
                pe.wait_ge(cout_ready, t + 1)
                transposes(("coutT", t), [cout[:, t, P * j:P * j + P] for j in range(4)])
            for name in ("qd", "kd"):
                for pair in range(2):
                    wait_emptied(pe, (name, 0, pair))
            for t in range(NT):
                wait_emptied(pe, ("vd", 0, t))
            attention(attD)
            for t in range(NT):
                wait_emptied(pe, ("coutT", t))
            wait_turned(attD)
            token_major_chunks("odout", 2, oT)
            feed_forward(1)
            assert filled_so_far[0] == len(FILLS)

        @block.scalar
        def _(act):
            steps = [0]

            def step(ins):
                steps[0] += 1
                ins.then_inc(scalar_step, 1)
                act.wait_ge(scalar_step, steps[0])

            def empty(name, dst, src=None, func=ACT.Copy):
                b = wait_filled(act, name)
                nc.scalar.activation(dst, b if src is None else src(b), func).then_inc(emptied_sem(name), 1)

            def root(src, junk, total, column, width):
                step(nc.scalar.activation(junk, src, ACT.Square, accum_out=total))
                nc.scalar.activation(rstd[:, column:column + 1], total, ACT.Sqrt, bias=eps,
                                     scale=1.0 / width).then_inc(root_ready, 1)

            def norm_roots(after):
                for t in range(NT):
                    for name in (after(t) if after else ()):
                        wait_emptied(act, name)
                    root(x[:, t, :], xn[:, t, :], ssq[:, t:t + 1], t, D)

            def sums(name):
                return lambda t: [(name, i, t) for i in range(2)]

            def copies(name, t_or_pair, dst):
                for j in range(2):
                    empty((name, t_or_pair, j), dst(j))

            def attention(a):
                def exponentials(h):
                    n = first_head[a.name] + h
                    if h >= 2:
                        act.wait_ge(bank_filled, FILL_NO[(a.name, "T", h - 2)] + 1)
                    act.wait_ge(nmax_ready, n + 1)
                    src = bank((a.name, "S", h)) if a.table is None else sc_sb[:, h % 2, :]
                    for t in range(NT):
                        last = nc.scalar.activation(pr_sb[:, h % 2, S * t:S * t + S], src[:, S * t:S * t + S], ACT.Exp,
                                                    bias=nmax[:, h, t:t + 1], scale=a.scale if a.table is None else 1.0,
                                                    accum_out=den[:, h, t:t + 1])
                    last.then_inc(emptied_sem((a.name, "S", h)) if a.table is None else probs_ready, 1)

                def turned(h):
                    if h >= 2:
                        act.wait_ge(pv_done, first_head[a.name] + h - 1)
                    empty((a.name, "T", h), pt_sb[:, h % 2, :])

                for h in range(a.heads):
                    exponentials(h)
                    if a.sinks and h % 8 == 7:
                        act.wait_ge(nmaxs_ready, h // 8 + 1)
                        w = sinkw[:, h - 7:h + 1, :]
                        nc.scalar.activation(w, w, ACT.Exp).then_inc(sinkw_ready, 1)
                    if h:
                        turned(h - 1)
                turned(a.heads - 1)
                for g in range(a.heads // 8):
                    for t in range(NT):
                        c = a.column(g) // P
                        empty((a.name, "OT", g, t), oT[:, c:c + 4, tile128(t)],
                              lambda b: b.rearrange("p (k n) -> p k n", k=4))

            def split_high(layer, q):
                wait_chunk(act, part_chunk(layer, q)[0])
                if q in (GU, GU + 1):
                    wait_part_output(layer)
                elif q >= 2:
                    wait_part_used(act, layer, q - 2)
                nc.scalar.activation(part_split(w_hi, layer, q), part_raw(layer, q), ACT.Copy).then_inc(hi_split, 1)

            def wait_part_output(layer):
                act.wait_ge(bank_filled, FILL_NO[(("evout", "odout")[layer], 1, 1)] + 1)

            def projections(layer, destination):
                split_high(layer, 0)
                split_high(layer, 1)
                for c, (name, i) in enumerate(PROJECTIONS[layer]):
                    if c < 4:
                        split_high(layer, 2 * c + 2)
                    if name in FEATURE_MAJOR:
                        dst = destination[name]
                        empty((name, i, 0), dst[:, 0:2, :].rearrange("p a b -> p (a b)"))
                        if c < 4:
                            split_high(layer, 2 * c + 3)
                        empty((name, i, 1), dst[:, 2:4, :].rearrange("p a b -> p (a b)"))
                    else:
                        if c < 4:
                            split_high(layer, 2 * c + 3)
                        for t in range(NT):
                            empty((name, i, t), destination[name][:, t, 512 * i:512 * i + 512],
                                  func=ACT.Gelu_apprx_tanh if name in ("uz", "vz") else ACT.Copy)
                    if layer and c == 2:
                        for t in range(NT):
                            act.wait_ge(vcen_ready, t + 1)
                            step(nc.scalar.activation(xn[:, t, 0:CW], vz[:, t, :], ACT.Square,
                                                      accum_out=ssq[:, t:t + 1]))
                            nc.scalar.activation(rstd[:, t:t + 1], ssq[:, t:t + 1], ACT.Sqrt, bias=eps,
                                                 scale=1.0 / CW).then_inc(vroot_ready, 1)

            def feed_forward(layer):
                name = "gu%d" % layer
                split_high(layer, GU)
                split_high(layer, GU + 1)
                for i in range(KF // 2):
                    split_high(layer, GU + 2 * i + 2)
                    if i >= 2:
                        act.wait_ge(gu_ready, KF // 2 * layer + i - 1)
                    b = wait_filled(act, (name, i, 0))
                    nc.scalar.activation(silu[:, i % 2, :], b, ACT.Silu).then_inc(emptied_sem((name, i, 0)), 1)
                    split_high(layer, GU + 2 * i + 3)
                for q in range(DOWN + 2, LAYER_PARTS):
                    split_high(layer, q)

            act.wait_ge(angle_ready, 1)
            nc.scalar.activation(angles[:, 2:4, :, :], angles[:, 0:2, :, :], ACT.Sin).then_inc(trig_ready, 1)
            act.wait_ge(x_landed, 16)
            act.wait_ge(eps_ready, 1)
            norm_roots(None)
            act.wait_ge(param_landed, 16)
            for i in range(4):
                if i >= 2:
                    wait_emptied(act, ("glu", i - 2, 0))
                b = wait_filled(act, ("glu", i, 1))
                for j in range(2):
                    m = 8 + 2 * i + j
                    last = nc.scalar.activation(glu_sig[:, i % 2, S * j:S * j + S], b[:, S * j:S * j + S], ACT.Sigmoid,
                                                bias=par_("b_glu")[:, m:m + 1])
                last.then_inc(emptied_sem(("glu", i, 1)), 1)
            for i in range(2):
                for t in range(NT):
                    empty(("q1", i, t), qkv[:, t, 512 * i:512 * i + 512])
            for t in range(NT):
                empty(("kv1", 0, t), qkv[:, t, 1024:1280], lambda b: b[:, 0:256])
            for i in range(4):
                for pair in range(2):
                    b = wait_filled(act, ("gate", i, pair))
                    for j in range(2):
                        m = 4 * i + 2 * pair + j
                        dst = (sgc if m < KD else sga)[:, m % KD, :]
                        last = nc.scalar.activation(dst, b[:, S * j:S * j + S], ACT.Sigmoid,
                                                    bias=par_("b_gate")[:, m:m + 1])
                    last.then_inc(emptied_sem(("gate", i, pair)), 1)
            for t in range(NT):
                for hf in range(2):
                    empty(("q1T", t, hf), q1T[:, 4 * hf:4 * hf + 4, tile128(t)],
                          lambda b: b.rearrange("p (k n) -> p k n", k=4))
            empty(("k1T",), k1T.rearrange("p n s -> p (n s)"))
            wait_emptied(act, ("mean",))
            nc.scalar.activation(ysq, y, ACT.Square).then_inc(ysq_ready, 1)
            b = wait_filled(act, ("var",))
            nc.scalar.activation(sc_sb[:, 0, 0:S], b[:, 0:S], ACT.Sqrt, bias=eps,
                                 scale=1.0 / D).then_inc(emptied_sem(("var",)), 1)
            act.wait_ge(ynorm_ready, 1)
            for m in range(KD):
                last = nc.scalar.activation(y[:, m, :], y[:, m, :], ACT.Silu, bias=par_("ln_b")[:, m:m + 1],
                                            scale=par_("ln_g")[:, m:m + 1])
            last.then_inc(silu_ready, 1)
            attention(att1)
            norm_roots(sums("wout"))
            for kind, i in QUERY_ORDER:
                if kind == "pq" and i >= 2:
                    act.wait_ge(bank_filled, FILL_NO[("sc", i - 2, 1)] + 1)
                for j in range(2):
                    if kind == "pq":
                        empty((kind, i, j), qpT[:, i % 2, 2 * j:2 * j + 2, :].rearrange("p a b -> p (a b)"))
                    else:
                        empty((kind, i, j), scores[:, j, 512 * i:512 * i + 512])

            def gate_exp(unit):
                act.wait_ge(shifted_ready, unit + 1)
                g = gates[:, 2 * TOPK * unit:2 * TOPK * (unit + 1)]
                nc.scalar.activation(g, g, ACT.Exp).then_inc(best_exp_ready, 1)

            gate_exp(0)
            for unit in range(UNITS):
                if unit + 1 < UNITS:
                    gate_exp(unit + 1)
                with act.Fori(0, UNIT_GROUPS // 4) as r:
                    for b in range(4):
                        act.wait_ge(dots_ready, r * 4 + (UNIT_GROUPS * unit + b + 1))
                        nc.scalar.activation(acts[:, b, :], dots[:, b, :], ACT.Gelu).then_inc(acts_ready, 1)
            for t in range(NT):
                act.wait_ge(rows_used, SLOTS // 2 * (t + 1))
                root(x[:, t, :], xn[:, t, :], ssq[:, t:t + 1], t, D)
            for t in range(NT):
                act.wait_ge(x_normed, t + 1)
                root(x[:, t, :], xn[:, t, :], ssq[:, t:t + 1], t, D)
            projections(0, {"qa": qaT, "ka": kaT, "va": va, "cqkv": cqkv})
            for t in range(NT):
                for i, (lo, hi) in enumerate(((0, QRANK), (QRANK, D))):
                    wait_emptied(act, ("cqkv", 1, t))
                    root(cqkv[:, t, lo:hi], xn[:, t, lo:hi], ssq[:, i:i + 1], 2 * i + t, hi - lo)
            attention(attA)
            for t in range(NT):
                empty(("kpe", 0, t), kpe[:, t, :], lambda b: b[:, 0:ROPE2])
            for t in range(NT):
                empty(("uqa", 0, t), uq[:, t, 0:512])
            for t in range(NT):
                empty(("uqb", 0, t), uq[:, t, 512:QRANK], lambda b: b[:, 0:256])
            for i in range(2):
                for t in range(NT):
                    empty(("ukv", i, t), ukv[:, t, 512 * i:512 * i + 512])
            for n, dst in (("qmT", qmT), ("kmT", kmT)):
                for t in range(NT):
                    for hf in range(2):
                        empty((n, t, hf), dst[0:QK2, 4 * hf:4 * hf + 4, tile128(t)],
                              lambda b: b[0:QK2, :].rearrange("p (k n) -> p k n", k=4))
            attention(attB)
            norm_roots(sums("evout"))

            feed_forward(0)
            norm_roots(lambda t: [("down0", n, t) for n in range(2)])
            projections(1, {"uz": uz, "vz": vz, "qd": qdT, "kd": kdT, "vd": vd})
            for t in range(NT):
                empty(("coutT", t), oT[:, 0:4, tile128(t)], lambda b: b.rearrange("p (k n) -> p k n", k=4))
            attention(attD)
            norm_roots(sums("odout"))
            feed_forward(1)
            norm_roots(lambda t: [("down1", n, t) for n in range(2)])

        @block.vector
        def _(dve):
            steps = [0]

            def mark(ins):
                steps[0] += 1
                ins.then_inc(vector_step, 1)
                return steps[0]

            def after(n):
                dve.wait_ge(vector_step, n)

            def link(ins):
                after(mark(ins))

            V = nc.vector

            def normed(name, src=None, dst=None, rows_=None, signal=None):
                for t in range(NT):
                    dve.wait_ge(root_ready, roots_before[name] + t + 1)
                    r = rstd[:, t:t + 1]
                    link(V.reciprocal(r, r))
                    d = (xn if dst is None else dst)[:, t, :]
                    if rows_ is None:
                        ins = V.tensor_scalar(d, x[:, t, :], r, None, ALU.mult)
                    else:
                        ins = V.scalar_tensor_tensor(d, x[:, t, :], r, rows_, ALU.mult, ALU.mult)
                    ins.then_inc(xn_ready if signal is None else signal, 1)

            def gained(name, dst):
                g = par_(gain_of[name]) if name in gain_of else None
                for t in range(NT):
                    for hf in range(2):
                        b = wait_filled(dve, (name, t, hf)).rearrange("p (k n) -> p k n", k=4)
                        d = dst[:, 4 * hf:4 * hf + 4, tile128(t)]
                        if g is None:
                            ins = V.tensor_copy(d, b)
                        else:
                            ins = V.tensor_tensor(d, b, g[:, 4 * hf:4 * hf + 4].unsqueeze(2).to_broadcast([P, 4, P]),
                                                  ALU.mult)
                        ins.then_inc(emptied_sem((name, t, hf)), 1)

            def add_to_x(name):
                for i in range(2):
                    for t in range(NT):
                        b = wait_filled(dve, (name, i, t))
                        d = x[:, t, 512 * i:512 * i + 512]
                        V.tensor_tensor(d, d, b, ALU.add).then_inc(emptied_sem((name, i, t)), 1)

            def attention(a):
                def divide(g):
                    dg = den[:, 8 * g:8 * g + 8, :]
                    wait_probs(dve, a, 8 * g + 7)
                    if a.sinks:
                        dve.wait_ge(sinkw_ready, g + 1)
                        link(V.tensor_tensor(dg, dg, sinkw[:, 8 * g:8 * g + 8, :], ALU.add))
                    link(V.reciprocal(dg, dg))
                    dve.wait_ge(pv_done, first_head[a.name] + 8 * g + 8)
                    for t in range(NT):
                        c = a.column(g)
                        V.tensor_tensor(otm[:, t, c:c + 512].rearrange("p (h d) -> p h d", h=8),
                                        psum[:, RB + t, :].rearrange("p (h d) -> p h d", h=8),
                                        dg[:, :, t].unsqueeze(2).to_broadcast([P, 8, HD]),
                                        ALU.mult).then_inc(o_emptied, 1)

                for h in range(a.heads):
                    n = first_head[a.name] + h
                    b = wait_filled(dve, (a.name, "S", h))
                    if a.table is not None:
                        if h >= 2:
                            wait_probs(dve, a, h - 2)
                        for t in range(NT):
                            ins = V.scalar_tensor_tensor(sc_sb[:, h % 2, S * t:S * t + S], b[:, S * t:S * t + S],
                                                         a.scale, a.table(h)[:, P - P * t:P - P * t + S],
                                                         ALU.mult, ALU.add)
                        ins.then_inc(emptied_sem((a.name, "S", h)), 1)
                        wait_emptied(dve, (a.name, "S", h))
                        src = sc_sb[:, h % 2, :]
                    else:
                        src = b
                    m = nmax[:, h, :]
                    ins = V.tensor_reduce(m, src.rearrange("p (t k) -> p t k", t=NT), AX, ALU.max, negate=True)
                    if a.table is None:
                        link(ins)
                        ins = V.tensor_scalar(m, m, a.scale, None, ALU.mult)
                    if a.sinks:
                        link(ins)
                        ins = V.tensor_scalar(m, m, nsink[:, h:h + 1], None, ALU.min)
                    ins.then_inc(nmax_ready, 1)
                    if a.sinks and h % 8 == 7:
                        dve.wait_ge(nmax_ready, n + 1)
                        V.tensor_tensor(sinkw[:, h - 7:h + 1, :], nmax[:, h - 7:h + 1, :],
                                        nsink[:, h - 7:h + 1].unsqueeze(2).to_broadcast([P, 8, NT]),
                                        ALU.subtract).then_inc(nmaxs_ready, 1)
                    if h == 8:
                        divide(0)
                divide(a.heads // 8 - 1)

            def split_low(layer, q):
                dve.wait_ge(hi_split, LAYER_PARTS * layer + q + 1)
                V.tensor_tensor(part_split(w_lo, layer, q), part_raw(layer, q),
                                part_split(w_hi, layer, q).bitcast(F32), ALU.subtract).then_inc(lo_split, 1)

            def gained_halves(name, high, low):
                gained(name, hT)
                for t in range(NT):
                    for hf in range(2):
                        cols = (slice(None), slice(4 * hf, 4 * hf + 4), tile128(t))
                        wait_emptied(dve, (name, t, hf))
                        link(V.tensor_copy(high[cols], hT[cols]))
                        V.tensor_tensor(low[cols], hT[cols], high[cols].bitcast(F32), ALU.subtract
                                        ).then_inc(h_split, 1)

            def feed_forward(layer):
                name = "ffn%d" % layer
                normed(name)
                split_low(layer, GU)
                split_low(layer, GU + 1)
                gained_halves(name, h_hi, h_lo)
                name = "gu%d" % layer
                for i in range(KF // 2):
                    split_low(layer, GU + 2 * i + 2)
                    wait_emptied(dve, (name, i, 0))
                    b = wait_filled(dve, (name, i, 1))
                    g = silu[:, i % 2, :]
                    hi, lo = (v[:, 2 * i:2 * i + 2, :].rearrange("p a b -> p (a b)") for v in (gu_hi, gu_lo))
                    V.tensor_tensor(g, g, b, ALU.mult).then_inc(emptied_sem((name, i, 1)), 1)
                    split_low(layer, GU + 2 * i + 3)
                    wait_emptied(dve, (name, i, 1))
                    link(V.tensor_copy(hi, g))
                    V.tensor_tensor(lo, g, hi.bitcast(F32), ALU.subtract).then_inc(gu_ready, 1)
                for q in range(DOWN + 2, LAYER_PARTS):
                    split_low(layer, q)
                add_to_x("down%d" % layer)

            V.memset(eps, EPS).then_inc(eps_ready, 1)
            link(V.memset(u[:, :, 0:TAPS - 1], 0.0))
            dve.wait_ge(pos_landed, 16)
            dve.wait_ge(const_landed, 16)
            link(V.tensor_copy(posf, pos_i[:, :]))
            raw, turns = angles[:, 0, :, :], angles[:, 1, :, :]
            for t in range(NT):
                n = mark(V.tensor_scalar(angles[:, 0, t, :], c_("inv"), posf[:, t:t + 1], None, ALU.mult))
            after(n)
            link(V.tensor_scalar(turns, raw, float(1 / (2 * np.pi)), None, ALU.mult))
            link(V.tensor_scalar(turns, turns, 12582912.0, None, ALU.add))
            link(V.tensor_scalar(turns, turns, -12582912.0, None, ALU.add))
            c1 = 6.28125
            c2 = float(np.float32(2 * np.pi - c1)) - float(np.float32(2 * np.pi - c1)) % 2.0 ** -20
            c3 = float(2 * np.pi - c1 - c2)
            for c in (c1, c2, c3):
                link(V.scalar_tensor_tensor(raw, turns, -c, raw, ALU.mult, ALU.add))
            lim = float(np.nextafter(np.float32(np.pi), np.float32(0)))
            link(V.tensor_scalar(raw, raw, lim, -lim, ALU.min, ALU.max))
            link(V.scalar_tensor_tensor(turns, raw, -1.0, raw, ALU.mult, ALU.min))
            V.tensor_scalar(turns, turns, float(np.pi / 2), None, ALU.add).then_inc(angle_ready, 1)
            b = wait_filled(dve, ("t5",))
            V.tensor_tensor(t5vec, b[0:HEADS2, :], t5ln, ALU.add).then_inc(emptied_sem(("t5",)), 1)

            normed("N1")
            dve.wait_ge(param_landed, 16)
            gained("N1", hT)

            def conv_pair(i):
                for w in range(TAPS):
                    for m in (2 * i, 2 * i + 1):
                        src, tap = u[:, m, w:w + S], conv_w[:, m, w:w + 1]
                        if w == 0:
                            n = mark(V.tensor_scalar(y[:, m, :], src, tap, par_("conv_b")[:, m:m + 1],
                                                     ALU.mult, ALU.add))
                        elif w == TAPS - 1 and m == 2 * i + 1:
                            after(steps[0] - 1)
                            V.scalar_tensor_tensor(y[:, m, :], src, tap, y[:, m, :], ALU.mult, ALU.add
                                                   ).then_inc(conv_ready, 1)
                        else:
                            after(steps[0] - 1)
                            n = mark(V.scalar_tensor_tensor(y[:, m, :], src, tap, y[:, m, :], ALU.mult, ALU.add))
                return n

            for i in range(4):
                wait_emptied(dve, ("glu", i, 1))
                b = wait_filled(dve, ("glu", i, 0))
                for j in range(2):
                    m = 2 * i + j
                    ins = V.scalar_tensor_tensor(u[:, m, TAPS - 1:], b[:, S * j:S * j + S], par_("b_glu")[:, m:m + 1],
                                                 glu_sig[:, i % 2, S * j:S * j + S], ALU.add, ALU.mult)
                ins.then_inc(emptied_sem(("glu", i, 0)), 1)
                if i:
                    conv_pair(i - 1)
                wait_emptied(dve, ("glu", i, 0))
            dve.wait_ge(row_landed, 16)
            for t in range(NT):
                for name in (("q1", 0, t), ("q1", 1, t), ("kv1", 0, t)):
                    wait_emptied(dve, name)
            link(V.tensor_tensor(qkv, qkv, row_("b_qkv").unsqueeze(1).to_broadcast([P, NT, 1280]), ALU.add))
            dve.wait_ge(trig_ready, 1)
            dve.wait_ge(t5_stored, 16)
            dve.wait_ge(rpb_stored, 16 * RPB_ROWS)
            for t in range(NT):
                heads = qkv[:, t, 0:18 * HD].rearrange("p (h d) -> p h d", d=HD)
                turned = qkr[:, t, :].rearrange("p (h d) -> p h d", d=HD)
                sin = angles[:, 2, t, :].unsqueeze(1).to_broadcast([P, 18, 32])
                cos = angles[:, 3, t, :].unsqueeze(1).to_broadcast([P, 18, 32])
                lo, hi = heads[:, :, 0:32], heads[:, :, 32:64]
                V.tensor_tensor(rope_tmp[:, 0], lo, cos, ALU.mult)
                V.tensor_tensor(rope_tmp[:, 1], hi, sin, ALU.mult)
                V.tensor_tensor(rope_tmp[:, 2], hi, cos, ALU.mult)
                link(V.tensor_tensor(rope_tmp[:, 3], lo, sin, ALU.mult))
                V.tensor_tensor(turned[:, :, 0:32], rope_tmp[:, 0], rope_tmp[:, 1], ALU.subtract)
                link(V.tensor_tensor(turned[:, :, 32:64], rope_tmp[:, 2], rope_tmp[:, 3], ALU.add))
                for c in range(2):
                    ins = V.tensor_copy(kdup[:, t, :, c, :], turned[:, 16:18, :])
                ins.then_inc(rope_ready, 1)
            conv_pair(3)
            b = wait_filled(dve, ("mean",))
            V.scalar_tensor_tensor(y, b[:, 0:S].unsqueeze(1).to_broadcast([P, KD, S]), -1.0 / D, y,
                                   ALU.mult, ALU.add).then_inc(emptied_sem(("mean",)), 1)
            wait_emptied(dve, ("var",))
            dev = sc_sb[:, 0, 0:S]
            link(V.reciprocal(dev, dev))
            V.tensor_tensor(y, y, dev.unsqueeze(1).to_broadcast([P, KD, S]), ALU.mult).then_inc(ynorm_ready, 1)
            link(V.tensor_scalar(nsink, row_("sinks"), -1.0, None, ALU.mult))
            dve.wait_ge(ynorm_ready, 1)
            attention(att1)
            for name, g in (("convout", sgc), ("attno", sga)):
                for i in range(2):
                    for pair in range(2):
                        b = wait_filled(dve, (name, i, pair))
                        m = 4 * i + 2 * pair
                        wait_emptied(dve, ("gate", i + (2 if name == "attno" else 0), pair))
                        d = g[:, m:m + 2, :].rearrange("p a b -> p (a b)")
                        V.tensor_tensor(d, d, b, ALU.mult).then_inc(emptied_sem((name, i, pair)), 1)
            for name in ("convout", "attno"):
                for i in range(2):
                    for pair in range(2):
                        wait_emptied(dve, (name, i, pair))
            V.tensor_tensor(hT[:, :, :], sgc, sga, ALU.add).then_inc(merged_ready, 1)
            add_to_x("wout")
            normed("N2", rows_=row_("norm2"))
            gained("N2", hT)

            def top16(src, values, indices):
                link(V.max(values[:, 0:8], src))
                V.max_index(indices[:, 0:8], values[:, 0:8], src)
                link(V.match_replace(src, values[:, 0:8], src, -3.0e38))
                link(V.max(values[:, 8:16], src))
                link(V.max_index(indices[:, 8:16], values[:, 8:16], src))

            def select(unit):
                t, i = unit // (PH // 2), unit % (PH // 2)
                wait_emptied(dve, ("sc", i, t))
                for m in range(4):
                    c = 512 * i + NKEYS * m
                    top16(scores[:, t, c:c + NKEYS], topv[:, m, :], topi[:, m, :])
                link(V.tensor_copy(topf[:, :, :], topi[:, :, :]))
                tv = topv[:, :, :].rearrange("p (h c) k -> p h c k", c=2)
                tf = topf[:, :, :].rearrange("p (h c) k -> p h c k", c=2)
                shape = [P, 2, TOPK, TOPK]
                grid = cand.rearrange("p h (i j) -> p h i j", i=TOPK)
                link(V.tensor_tensor(grid, tv[:, :, 0, :].unsqueeze(3).to_broadcast(shape),
                                     tv[:, :, 1, :].unsqueeze(2).to_broadcast(shape), ALU.add))
                for h in range(2):
                    top16(cand[:, h, :], best[:, h, :], bpos[:, h, :])
                V.tensor_scalar(bdig[:, 0], bpos[:, :, :], 4, None, ALU.logical_shift_right)
                link(V.tensor_scalar(bdig[:, 1], bpos[:, :, :], 15, None, ALU.bitwise_and))
                link(V.tensor_copy(bdigf[:, :, :, :], bdig[:, :, :, :]))
                iota = c_("iota").unsqueeze(1).unsqueeze(1).to_broadcast(shape)
                for c in range(2):
                    link(V.tensor_tensor(grid, bdigf[:, c].unsqueeze(3).to_broadcast(shape), iota, ALU.is_equal))
                    link(V.tensor_tensor(grid, grid, tf[:, :, c, :].unsqueeze(2).to_broadcast(shape), ALU.mult))
                    link(V.tensor_reduce(hits[:, c], grid, AX, ALU.add))
                cols = slice(2 * TOPK * unit, 2 * TOPK * (unit + 1))
                V.scalar_tensor_tensor(experts[:, cols], hits[:, 0].rearrange("p h k -> p (h k)"), float(NKEYS),
                                       hits[:, 1].rearrange("p h k -> p (h k)"), ALU.mult, ALU.add
                                       ).then_inc(selected, 1)
                g = gates[:, cols].rearrange("p (h k) -> p h k", h=2)
                V.tensor_tensor(g, best[:, :, :], best[:, :, 0:1].to_broadcast([P, 2, TOPK]), ALU.subtract
                                ).then_inc(shifted_ready, 1)

            def weights(unit):
                g = gates[:, 2 * TOPK * unit:2 * TOPK * (unit + 1)].rearrange("p (h k) -> p h k", h=2)
                dve.wait_ge(best_exp_ready, unit + 1)
                link(V.tensor_reduce(gsum[:, :], g, AX, ALU.add))
                link(V.reciprocal(gsum[:, :], gsum[:, :]))
                link(V.tensor_tensor(g, g, gsum[:, :].unsqueeze(2).to_broadcast([P, 2, TOPK]), ALU.mult))

            def dot(t, n, b, r, k):
                if k == 0:
                    dve.wait_ge(rows_landed[b], r * 32 + 32 * (n // 4 + 1))
                row_u = gath[:, 2 * b + k, 0:D]
                ins = V.tensor_tensor_reduce(out=row_u, in0=row_u, in1=xn[:, t, :], scale=1.0,
                                             scalar=0.0, op0=ALU.mult, op1=ALU.add, accum_out=dots[:, b, k:k + 1])
                if k == 1:
                    ins.then_inc(dots_ready, 1)

            def weigh(n, b, r, base):
                dve.wait_ge(acts_ready, r * 4 + (n + 1))
                V.tensor_tensor(coef[:, b, :], acts[:, b, :], gates[:, bass.ds(r * 8 + 2 * n, 2)], ALU.mult
                                ).then_inc(vector_step, 1)
                dve.wait_ge(vector_step, r * 8 + (base + 2 * b + 1))

            def add_row(t, b, r, k, base):
                ins = V.scalar_tensor_tensor(x[:, t, :], gath[:, 2 * b + k, D:2 * D], coef[:, b, k:k + 1], x[:, t, :],
                                             ALU.mult, ALU.add)
                if k == 0:
                    ins.then_inc(vector_step, 1)
                    dve.wait_ge(vector_step, r * 8 + (base + 2 * b + 2))
                else:
                    ins.then_inc(rows_used, 1)

            def consume(unit):
                t, first, base = unit // (PH // 2), UNIT_GROUPS * unit, steps[0]

                def group(b, r, ahead):
                    if ahead:
                        dot(t, first + b + 1, (b + 1) % 4, r, 0)
                    weigh(first + b, b, r, base)
                    add_row(t, b, r, 0, base)
                    if ahead:
                        dot(t, first + b + 1, (b + 1) % 4, r, 1)
                    add_row(t, b, r, 1, base)
                    dve.wait_ge(rows_used, r * 4 + (first + b + 1))

                dot(t, first, 0, 0, 0)
                dot(t, first, 0, 0, 1)
                with dve.Fori(0, UNIT_GROUPS // 4 - 1) as r:
                    for b in range(4):
                        group(b, r, True)
                for b in range(4):
                    group(b, UNIT_GROUPS // 4 - 1, b < 3)
                steps[0] = base + 2 * UNIT_GROUPS

            select(0)
            for unit in range(UNITS):
                if unit + 1 < UNITS:
                    select(unit + 1)
                weights(unit)
                consume(unit)

            normed("F1", dst=x, rows_=row_("final1"), signal=x_normed)
            normed("mix0")
            split_low(0, 0)
            split_low(0, 1)
            gained_halves("mix0", p_hi, p_lo)
            for q in range(2, GU):
                split_low(0, q)
            for t in range(NT):
                for i, (lo, hi) in enumerate(((0, QRANK), (QRANK, D))):
                    c = 2 * i + t
                    dve.wait_ge(root_ready, roots_before["cT"] + 2 * t + i + 1)
                    link(V.reciprocal(rstd[:, c:c + 1], rstd[:, c:c + 1]))
                    ins = V.tensor_scalar(cqkv[:, t, lo:hi], cqkv[:, t, lo:hi], rstd[:, c:c + 1], None, ALU.mult)
                ins.then_inc(xn_ready, 1)
            dve.wait_ge(taba_landed, 16)
            attention(attA)
            gained("cT", cT)
            for t in range(NT):
                for name in (("kpe", 0, t), ("uqa", 0, t), ("uqb", 0, t), ("ukv", 0, t), ("ukv", 1, t)):
                    wait_emptied(dve, name)
                cos = c_("cos2")[:, 16 * t:16 * t + 16]
                sin = c_("sin2")[:, 16 * t:16 * t + 16]
                qh = uq[:, t, :].rearrange("p (h d) -> p h d", h=HEADS2)
                kh = km[:, t, :].rearrange("p (h d) -> p h d", h=HEADS2)
                eight = [P, HEADS2, 16]
                tmp = xn[:, t, 0:640].rearrange("p (a h d) -> p a h d", a=5, h=HEADS2)
                lo, hi = qh[:, :, NOPE:NOPE + 16], qh[:, :, NOPE + 16:QK2]
                cb, sb_ = cos.unsqueeze(1).to_broadcast(eight), sin.unsqueeze(1).to_broadcast(eight)
                V.tensor_tensor(tmp[:, 0], lo, cb, ALU.mult)
                V.tensor_tensor(tmp[:, 1], hi, sb_, ALU.mult)
                V.tensor_tensor(tmp[:, 2], lo, sb_, ALU.mult)
                V.tensor_tensor(tmp[:, 3], hi, cb, ALU.mult)
                ktmp = tmp[:, 4]
                klo, khi = kpe[:, t, 0:16], kpe[:, t, 16:32]
                V.tensor_tensor(ktmp[:, 0, :], klo, cos, ALU.mult)
                V.tensor_tensor(ktmp[:, 1, :], khi, sin, ALU.mult)
                V.tensor_tensor(ktmp[:, 2, :], klo, sin, ALU.mult)
                link(V.tensor_tensor(ktmp[:, 3, :], khi, cos, ALU.mult))
                V.tensor_tensor(lo, tmp[:, 0], tmp[:, 1], ALU.subtract)
                V.tensor_tensor(hi, tmp[:, 2], tmp[:, 3], ALU.add)
                V.tensor_tensor(kh[:, :, NOPE:NOPE + 16], ktmp[:, 0:1, :].to_broadcast(eight),
                                ktmp[:, 1:2, :].to_broadcast(eight), ALU.subtract)
                V.tensor_tensor(kh[:, :, NOPE + 16:QK2], ktmp[:, 2:3, :].to_broadcast(eight),
                                ktmp[:, 3:4, :].to_broadcast(eight), ALU.add)
                V.tensor_copy(kh[:, :, 0:NOPE], ukv[:, t, :].rearrange("p (h d) -> p h d", h=HEADS2)[:, :, 0:NOPE]
                              ).then_inc(rope_ready, 1)
            attention(attB)
            add_to_x("evout")

            feed_forward(0)
            normed("mix1")
            split_low(1, 0)
            split_low(1, 1)
            gained_halves("mix1", p_hi, p_lo)
            for q in range(2, 7):
                split_low(1, q)
            for t in range(NT):
                wait_emptied(dve, ("vz", 0, t))
                link(V.tensor_reduce(vsum[:, t:t + 1], vz[:, t, :], AX, ALU.add, negate=True))
                link(V.tensor_scalar(vsum[:, t:t + 1], vsum[:, t:t + 1], 1.0 / CW, None, ALU.mult))
                V.tensor_scalar(vz[:, t, :], vz[:, t, :], vsum[:, t:t + 1], None, ALU.add).then_inc(vcen_ready, 1)
            split_low(1, 7)
            split_low(1, 8)
            dve.wait_ge(late_landed, 32)
            gain = row[:, LATE["v_gain"][0]:LATE["v_gain"][1]]
            for t in range(NT):
                dve.wait_ge(vroot_ready, t + 1)
                dve.wait_ge(vcen_ready, t + 1)
                link(V.reciprocal(rstd[:, t:t + 1], rstd[:, t:t + 1]))
                V.scalar_tensor_tensor(vz[:, t, :], vz[:, t, :], rstd[:, t:t + 1], gain, ALU.mult, ALU.mult
                                       ).then_inc(vn_ready, 1)
            split_low(1, 9)
            for t in range(NT):
                b = wait_filled(dve, ("gating", t)).rearrange("p (g c) -> p g c", g=8)
                co = cout[:, t, :].rearrange("p (g c) -> p g c", g=8)
                V.tensor_tensor(co, b, par_("b_s").unsqueeze(2).to_broadcast([P, 8, 64]), ALU.add
                                ).then_inc(emptied_sem(("gating", t)), 1)
                wait_emptied(dve, ("gating", t))
                wait_emptied(dve, ("uz", 0, t))
                V.tensor_tensor(cout[:, t, :], cout[:, t, :], uz[:, t, :], ALU.mult).then_inc(cout_ready, 1)
            dve.wait_ge(tabd_ready, 1)
            attention(attD)
            add_to_x("odout")
            feed_forward(1)
            normed("F2", rows_=row[:, LATE["final2"][0]:LATE["final2"][1]], signal=out_ready)



def t5_bucket(rel):
    nb, max_exact = 16, 8
    n = np.abs(rel)
    large = max_exact + (np.log(np.maximum(n, 1) / max_exact) / np.log(1024 / max_exact) * (nb - max_exact)).astype(np.int64)
    return (rel > 0) * nb + np.where(n < max_exact, n, np.minimum(large, nb - 1))


def shape_constants():
    c = np.zeros((P, NCONST), np.float32)

    def put(name, v):
        c[:, CONST[name][0]:CONST[name][1]] = v
    p = np.arange(P)[:, None]
    put("ident", np.eye(P))
    put("ones", 1.0)
    put("inv", np.power(np.float32(10000.0), -(np.arange(32, dtype=np.float32) * np.float32(2.0) / np.float32(64)))[None])
    rel = p - (np.arange(TABW)[None] - P)
    put("mask1", np.where((rel >= 0) & (rel < 128), 0.0, NEG))
    qc, kc = p % GRID, np.arange(GRID)[None]
    start = np.clip(qc - 8, 0, GRID - 16)
    put("namask", np.where((kc >= start) & (kc < start + 16), 0.0, NEG))
    inv = np.float32(1.0) / np.power(np.float32(10000.0), np.arange(0, ROPE2, 2, dtype=np.float32) / np.float32(ROPE2))
    ang = (np.arange(S, dtype=np.float32)[:, None] * inv[None]).reshape(NT, P, 16).transpose(1, 0, 2).reshape(P, 32)
    put("cos2", np.cos(ang))
    put("sin2", np.sin(ang))
    put("iota", np.arange(TOPK)[None])
    rel = np.arange(REL) - S
    t5 = np.zeros((32 + HEADS2, REL), np.float32)
    t5[t5_bucket(rel), np.arange(REL)] = 1.0
    count = (np.abs(rel) <= 64).astype(int) + (rel % 4 == 0) + (rel % 16 == 0)
    t5[32:] = np.where(count > 0, np.log(np.maximum(count, 1)), NEG)[None]
    return c, t5



def by_k(w):
    k, n = w.shape
    return w.reshape(k // P, P, n).transpose(1, 0, 2).reshape(P, -1)


def feature(v):
    return v.reshape(-1, P).T


def kernel(**inputs):
    import concourse.bacc as bacc
    from concourse.bass_utils import run_bass_kernel_spmd

    a = {k: np.asarray(v) for k, v in inputs.items()}
    w_in = a["w_in"][0]
    parts = {}
    for i in range(4):
        parts["glu", i] = by_k(np.concatenate([w_in[:, 256 * i:256 * i + 256], w_in[:, 1024 + 256 * i:1280 + 256 * i]], 1))
        parts["gate", i] = by_k(w_in[:, 3328 + 512 * i:3840 + 512 * i])
        parts["pq", i] = by_k(a["w_peer_q"][0][:, 512 * i:512 * i + 512])
    parts["kv1", 0] = by_k(w_in[:, 3072:3328])
    ev, od = a["ev_w_in_2"][0], a["od_w_in_2"][0]
    for i in range(2):
        c = slice(512 * i, 512 * i + 512)
        parts["q1", i] = by_k(w_in[:, 2048 + 512 * i:2560 + 512 * i])
        for name, w in (("convout", "w_conv_out"), ("attno", "w_attn_o"), ("wout", "w_out"), ("evout", "ev_w_out_2"),
                        ("odout", "od_w_out_2")):
            parts[name, i] = by_k(a[w][0][:, c])
        parts["cqkv", i] = by_k(ev[:, 1536 + 512 * i:2048 + 512 * i])
    keys = a["peer_sub_keys"][0].transpose(3, 0, 1, 2).reshape(P, -1)
    for i, name in enumerate(("qa", "ka", "va")):
        parts[name, 0] = by_k(ev[:, 512 * i:512 * i + 512])
    w_uq = a["ev_w_uq_2"][0]
    parts["kpe_uq", 0] = np.concatenate([by_k(ev[:, 2560:2592]), by_k(w_uq[:, 0:512])], 1)
    parts["uq_ukv", 0] = np.concatenate([by_k(w_uq[:, 512:768]), by_k(a["ev_w_ukv_2"][0])], 1)
    for i, name in enumerate(("uz", "vz", "qd", "kd", "vd")):
        parts[name, 0] = by_k(od[:, 512 * i:512 * i + 512])
    parts["ws", 0] = a["od_w_s_2"][0].transpose(2, 0, 1).reshape(P, -1)
    for layer in range(2):
        gu, down = a["ffn_w_gu_2"][layer], a["ffn_w_down_2"][layer]
        for i in range(KF // 2):
            parts["gu%d" % layer, i] = by_k(np.concatenate([gu[:, 256 * i:256 * i + 256],
                                                            gu[:, FF + 256 * i:FF + 256 * i + 256]], 1))
        for i in range(-(-KF // 4)):
            parts["down%d" % layer, i] = by_k(down[512 * i:512 * i + 512])
    for name, width in CHUNKS:
        assert parts[name].shape == (P, width), (name, parts[name].shape, width)
    stream = np.concatenate([np.ascontiguousarray(parts[name]).ravel() for name, _ in CHUNKS])

    params = np.concatenate([
        feature(a["norm1_g"][0]), feature(a["b_in"][0][0:2048]), feature(a["b_in"][0][3328:5376]),
        a["conv_w"][0].reshape(TAPS, KD, P).transpose(2, 1, 0).reshape(P, -1), feature(a["conv_b"][0]),
        feature(a["conv_ln_g"][0]), feature(a["conv_ln_b"][0]), feature(a["norm_mix_2"][0]),
        feature(a["norm_mix_2"][1]), feature(a["norm_ffn_2"][0]), feature(a["norm_ffn_2"][1]),
        feature(a["ev_q_gain_2"][0]), feature(a["ev_kv_gain_2"][0]), a["od_b_s_2"][0].T], 1)
    rows = np.concatenate([a["b_in"][0][2048:3328], a["attn_sinks"][0], a["norm2_g"][0], a["final_g"]])[None]
    late = np.concatenate([a["final_gain_2"], a["od_v_gain_2"][0]])[None]
    uv = np.concatenate([a["peer_u"][0], a["peer_v"][0]], 1)
    consts, t5 = shape_constants()
    arrays = {
        "stream": stream, "consts": consts, "t5const": t5, "params": params, "rows": rows, "late_rows": late,
        "x_in": a["x"].reshape(S, D), "positions": a["positions"].reshape(NT, P).T, "t5_in": a["t5_bias_2"],
        "rpb_in": a["od_rpb_2"][0], "uv": uv, "keys_in": keys,
    }
    nc = bacc.Bacc("TRN2", target_bir_lowering=False, num_devices=1)
    arrays = {k: np.ascontiguousarray(v) for k, v in arrays.items()}
    aps = {k: nc.dram_tensor(k, v.shape, mybir.dt.from_np(v.dtype), kind="ExternalInput").ap() for k, v in arrays.items()}
    out = nc.dram_tensor("out", (S, D), F32, kind="ExternalOutput").ap()
    build(nc, out=out, **aps)
    r = run_bass_kernel_spmd(nc, [arrays], core_ids=[0])
    return r.results[0]["out"].reshape(1, S, D)
```
